# Optimizing a Trainium2 kernel written in Bass

```python
import jax, jax.numpy as jnp
from jax import lax
import numpy as np
import math

D_MODEL = 1024
BATCH = 1
SEQ = 256
DEPTH = 2

PLE_DIM = 256
N_MIXERS = 2
D_FF = 2816
FFN_HALF = 0.5
MLA_HEADS = 16
MLA_Q_RANK = 512
MLA_KV_RANK = 256
MLA_NOPE = 64
MLA_ROPE = 32
MLA_V = 64
ROPE_THETA = 10000.0
FOX_HEADS = 16
FOX_HEAD_DIM = 64
Q_BLOCK = 128
EPS = 1e-6
N_MLA_LAYERS = (DEPTH + N_MIXERS - 1) // N_MIXERS
N_FOX_LAYERS = DEPTH // N_MIXERS


def rms_norm(x, g):
    xf = x.astype(jnp.float32)
    y = xf * lax.rsqrt(jnp.mean(xf * xf, axis=-1, keepdims=True) + EPS)
    return (y * g.astype(jnp.float32)).astype(x.dtype)

def swiglu(x, w_in, w_out):
    gate, up = jnp.split(x @ w_in, 2, axis=-1)
    return (jax.nn.silu(gate) * up) @ w_out

def rope(x, pos):
    r = x.shape[-1]
    inv_freq = ROPE_THETA ** (-jnp.arange(0, r, 2, dtype=jnp.float32) / r)
    ang = pos.astype(jnp.float32)[:, :, None, None] * inv_freq
    cos = jnp.cos(ang).astype(x.dtype)
    sin = jnp.sin(ang).astype(x.dtype)
    x1, x2 = jnp.split(x, 2, axis=-1)
    return jnp.concatenate([x1 * cos - x2 * sin, x1 * sin + x2 * cos], axis=-1)

def block_causal_attention(q, k, v, decay=None):
    b, s, h, dk = q.shape
    dv = v.shape[-1]
    nb = s // Q_BLOCK
    scale = dk ** -0.5
    qb = q.reshape(b, nb, Q_BLOCK, h, dk).transpose(1, 0, 2, 3, 4)
    blk = jnp.arange(nb)
    k_pos = jnp.arange(s)
    c_k = None if decay is None else decay.transpose(0, 2, 1)

    def attend(qi, i, c_qi):
        logits = jnp.einsum('bqhd,bkhd->bhqk', qi, k).astype(jnp.float32) * scale
        if c_qi is not None:
            logits = logits + c_qi[:, :, :, None] - c_k[:, :, None, :]
        q_pos = i * Q_BLOCK + jnp.arange(Q_BLOCK)
        mask = k_pos[None, :] <= q_pos[:, None]
        logits = jnp.where(mask[None, None], logits, -jnp.inf)
        probs = jax.nn.softmax(logits, axis=-1)
        return jnp.einsum('bhqk,bkhd->bqhd', probs.astype(v.dtype), v)

    if decay is None:
        out = lax.map(lambda a: attend(a[0], a[1], None), (qb, blk))
    else:
        c_qb = decay.reshape(b, nb, Q_BLOCK, h).transpose(1, 0, 3, 2)
        out = lax.map(lambda a: attend(a[0], a[1], a[2]), (qb, blk, c_qb))
    return out.transpose(1, 0, 2, 3, 4).reshape(b, s, h, dv)

def mla_mixer(hn, pos, w_in, g_q_lat, w_uq, g_kv_lat, w_ukv, g_qn, g_kn, w_o):
    b, s, _ = hn.shape
    z = hn @ w_in
    c_q = z[..., :MLA_Q_RANK]
    c_kv = z[..., MLA_Q_RANK:MLA_Q_RANK + MLA_KV_RANK]
    k_pe = z[..., MLA_Q_RANK + MLA_KV_RANK:]
    q = (rms_norm(c_q, g_q_lat) @ w_uq).reshape(b, s, MLA_HEADS, MLA_NOPE + MLA_ROPE)
    kv = (rms_norm(c_kv, g_kv_lat) @ w_ukv).reshape(b, s, MLA_HEADS, MLA_NOPE + MLA_V)
    k_nope, v = kv[..., :MLA_NOPE], kv[..., MLA_NOPE:]
    k_pe_h = jnp.broadcast_to(k_pe[:, :, None, :], (b, s, MLA_HEADS, MLA_ROPE))
    k = jnp.concatenate([k_nope, k_pe_h], axis=-1)
    q = rms_norm(q, g_qn)
    k = rms_norm(k, g_kn)
    q = jnp.concatenate([q[..., :MLA_NOPE], rope(q[..., MLA_NOPE:], pos)], axis=-1)
    k = jnp.concatenate([k[..., :MLA_NOPE], rope(k[..., MLA_NOPE:], pos)], axis=-1)
    o = block_causal_attention(q, k, v)
    return o.reshape(b, s, MLA_HEADS * MLA_V) @ w_o

def fox_mixer(hn, w_in, b_f, g_qn, g_kn, w_o):
    b, s, _ = hn.shape
    hd = FOX_HEADS * FOX_HEAD_DIM
    z = hn @ w_in
    q = z[..., :hd].reshape(b, s, FOX_HEADS, FOX_HEAD_DIM)
    k = z[..., hd:2 * hd].reshape(b, s, FOX_HEADS, FOX_HEAD_DIM)
    v = z[..., 2 * hd:3 * hd].reshape(b, s, FOX_HEADS, FOX_HEAD_DIM)
    f_logit = z[..., 3 * hd:].astype(jnp.float32) + b_f.astype(jnp.float32)
    log_f = jax.nn.log_sigmoid(f_logit)
    decay = jnp.cumsum(log_f, axis=1)
    q = rms_norm(q, g_qn)
    k = rms_norm(k, g_kn)
    o = block_causal_attention(q, k, v, decay)
    return o.reshape(b, s, hd) @ w_o

def first_inputs(seed: int = 0) -> dict:
    key = jax.random.key(seed)
    ks = iter(jax.random.split(key, 40))

    def dense(shape, fan_in):
        return jax.random.normal(next(ks), shape, jnp.float32) * (fan_in ** -0.5)

    def gain(shape):
        return 1.0 + 0.1 * jax.random.normal(next(ks), shape, jnp.float32)

    x = jax.random.normal(next(ks), (BATCH, SEQ, D_MODEL), jnp.float32)
    p = jax.random.normal(next(ks), (DEPTH, BATCH, SEQ, PLE_DIM), jnp.float32)
    positions = jnp.broadcast_to(jnp.arange(SEQ, dtype=jnp.int32), (BATCH, SEQ))
    na, nf = N_MLA_LAYERS, N_FOX_LAYERS
    fox_in = 3 * FOX_HEADS * FOX_HEAD_DIM + FOX_HEADS
    return {
        "x": x,
        "p": p,
        "positions": positions,
        "g_ffn1": gain((DEPTH, D_MODEL)),
        "g_mix": gain((DEPTH, D_MODEL)),
        "g_ffn2": gain((DEPTH, D_MODEL)),
        "g_ple": gain((DEPTH, D_MODEL)),
        "ffn1_w_in": dense((DEPTH, D_MODEL, 2 * D_FF), D_MODEL),
        "ffn1_w_out": dense((DEPTH, D_FF, D_MODEL), D_FF),
        "ffn2_w_in": dense((DEPTH, D_MODEL, 2 * D_FF), D_MODEL),
        "ffn2_w_out": dense((DEPTH, D_FF, D_MODEL), D_FF),
        "ple_w_proj": dense((DEPTH, PLE_DIM, D_MODEL), PLE_DIM),
        "ple_w_gate": dense((DEPTH, D_MODEL, D_MODEL), D_MODEL),
        "mla_w_in": dense((na, D_MODEL, MLA_Q_RANK + MLA_KV_RANK + MLA_ROPE), D_MODEL),
        "mla_g_q_lat": gain((na, MLA_Q_RANK)),
        "mla_w_uq": dense((na, MLA_Q_RANK, MLA_HEADS * (MLA_NOPE + MLA_ROPE)), MLA_Q_RANK),
        "mla_g_kv_lat": gain((na, MLA_KV_RANK)),
        "mla_w_ukv": dense((na, MLA_KV_RANK, MLA_HEADS * (MLA_NOPE + MLA_V)), MLA_KV_RANK),
        "mla_g_qn": gain((na, MLA_NOPE + MLA_ROPE)),
        "mla_g_kn": gain((na, MLA_NOPE + MLA_ROPE)),
        "mla_w_o": dense((na, MLA_HEADS * MLA_V, D_MODEL), MLA_HEADS * MLA_V),
        "fox_w_in": dense((nf, D_MODEL, fox_in), D_MODEL),
        "fox_b_f": jax.random.uniform(next(ks), (nf, FOX_HEADS), jnp.float32, 1.0, 4.0),
        "fox_g_qn": gain((nf, FOX_HEAD_DIM)),
        "fox_g_kn": gain((nf, FOX_HEAD_DIM)),
        "fox_w_o": dense((nf, FOX_HEADS * FOX_HEAD_DIM, D_MODEL), FOX_HEADS * FOX_HEAD_DIM),
    }

def first_block(x, p, positions, g_ffn1, g_mix, g_ffn2, g_ple,
              ffn1_w_in, ffn1_w_out, ffn2_w_in, ffn2_w_out, ple_w_proj, ple_w_gate,
              mla_w_in, mla_g_q_lat, mla_w_uq, mla_g_kv_lat, mla_w_ukv,
              mla_g_qn, mla_g_kn, mla_w_o,
              fox_w_in, fox_b_f, fox_g_qn, fox_g_kn, fox_w_o):
    h = x
    for i in range(DEPTH):
        h = h + FFN_HALF * swiglu(rms_norm(h, g_ffn1[i]), ffn1_w_in[i], ffn1_w_out[i])
        hn = rms_norm(h, g_mix[i])
        j = i // N_MIXERS
        if i % N_MIXERS == 0:
            h = h + mla_mixer(hn, positions, mla_w_in[j], mla_g_q_lat[j], mla_w_uq[j],
                              mla_g_kv_lat[j], mla_w_ukv[j], mla_g_qn[j], mla_g_kn[j],
                              mla_w_o[j])
        else:
            h = h + fox_mixer(hn, fox_w_in[j], fox_b_f[j], fox_g_qn[j], fox_g_kn[j],
                              fox_w_o[j])
        h = h + FFN_HALF * swiglu(rms_norm(h, g_ffn2[i]), ffn2_w_in[i], ffn2_w_out[i])
        gate = jax.nn.sigmoid(rms_norm(h, g_ple[i]) @ ple_w_gate[i])
        h = h + gate * (p[i] @ ple_w_proj[i])
    return h


DEPTH_2 = 1

BRANCH_W = D_MODEL // 2
POOL_WINDOWS = (2, 4, 8, 16)
N_POOL_GROUPS = len(POOL_WINDOWS)
POOL_GROUP_W = BRANCH_W // N_POOL_GROUPS
DILATED_GROUPS = ((128, 1), (512, 4), (2048, 16))
N_ATT_GROUPS = len(DILATED_GROUPS)
HEAD_DIM = 64
HEADS_PER_GROUP = BRANCH_W // HEAD_DIM
N_ATT_HEADS = N_ATT_GROUPS * HEADS_PER_GROUP
QKV_W = N_ATT_HEADS * HEAD_DIM
NUM_BUCKETS = 32
MAX_DISTANCE = 1024
IN_W = 2 * BRANCH_W + 3 * QKV_W + BRANCH_W + 2 * D_MODEL
RMS_EPS = 1e-6
NEG_INF = -1e30


def _rmsnorm(x, g):
    xf = x.astype(jnp.float32)
    r = lax.rsqrt(jnp.mean(xf * xf, axis=-1, keepdims=True) + RMS_EPS)
    return (xf * r).astype(x.dtype) * g

def _t5_bucket(rel):
    nb = NUM_BUCKETS // 2
    ret = (rel > 0).astype(jnp.int32) * nb
    n = jnp.abs(rel)
    max_exact = nb // 2
    nf = jnp.maximum(n, 1).astype(jnp.float32)
    large = max_exact + (jnp.log(nf / max_exact) / math.log(MAX_DISTANCE / max_exact)
                         * (nb - max_exact)).astype(jnp.int32)
    large = jnp.minimum(large, nb - 1)
    return ret + jnp.where(n < max_exact, n, large)

def _multiscale_pool(u, w_pool, pool_scale):
    B, S, _ = u.shape
    ug = u.reshape(B, S, N_POOL_GROUPS, POOL_GROUP_W)
    cs = jnp.cumsum(ug.astype(jnp.float32), axis=1)
    cs = jnp.concatenate([jnp.zeros_like(cs[:, :1]), cs], axis=1)
    pos = jnp.arange(S, dtype=jnp.int32)[:, None]
    half = jnp.array([w // 2 for w in POOL_WINDOWS], dtype=jnp.int32)[None, :]
    lo = jnp.maximum(pos - half, 0)
    hi = jnp.minimum(pos + half - 1, S - 1)
    gidx = jnp.arange(N_POOL_GROUPS, dtype=jnp.int32)[None, :]
    win_sum = cs[:, hi + 1, gidx] - cs[:, lo, gidx]
    count = (hi - lo + 1).astype(jnp.float32)[None, :, :, None]
    pooled = (win_sum / count).astype(u.dtype) - ug
    mixed = jnp.einsum('bsgc,gcd->bsgd', pooled, w_pool)
    return mixed.reshape(B, S, BRANCH_W) * pool_scale

def _dilated_attention(q, k, v, rel_bias):
    B, S = q.shape[0], q.shape[1]
    n_blocks = S // Q_BLOCK
    scale = 1.0 / math.sqrt(HEAD_DIM)
    cfg = []
    for g, (window, dil) in enumerate(DILATED_GROUPS):
        n_side = window // (2 * dil)
        offs = jnp.arange(-n_side, n_side + 1, dtype=jnp.int32) * dil
        bias = rel_bias[_t5_bucket(offs)][:, g * HEADS_PER_GROUP:(g + 1) * HEADS_PER_GROUP]
        cfg.append((offs, bias.T.astype(jnp.float32), k[:, :, g], v[:, :, g]))

    def block(i):
        s0 = i * Q_BLOCK
        qpos = s0 + jnp.arange(Q_BLOCK, dtype=jnp.int32)
        qb = lax.dynamic_slice_in_dim(q, s0, Q_BLOCK, axis=1).astype(jnp.float32) * scale
        lses, outs = [], []
        for g, (offs, bias, kg_all, vg_all) in enumerate(cfg):
            nk = offs.shape[0]
            kpos = qpos[:, None] + offs[None, :]
            valid = (kpos >= 0) & (kpos < S)
            kidx = jnp.clip(kpos, 0, S - 1).reshape(-1)
            kg = jnp.take(kg_all, kidx, axis=1).reshape(B, Q_BLOCK, nk, HEADS_PER_GROUP, HEAD_DIM)
            vg = jnp.take(vg_all, kidx, axis=1).reshape(B, Q_BLOCK, nk, HEADS_PER_GROUP, HEAD_DIM)
            s = jnp.einsum('bqhd,bqkhd->bhqk', qb[:, :, g], kg.astype(jnp.float32))
            s = s + bias[None, :, None, :]
            s = jnp.where(valid[None, None], s, NEG_INF)
            lse = jax.nn.logsumexp(s, axis=-1)
            p = jnp.exp(s - lse[..., None])
            outs.append(jnp.einsum('bhqk,bqkhd->bqhd', p, vg.astype(jnp.float32)))
            lses.append(lse)
        wts = jax.nn.softmax(jnp.stack(lses, axis=0), axis=0)
        wts = jnp.transpose(wts, (0, 1, 3, 2))[..., None]
        out = jnp.sum(wts * jnp.stack(outs, axis=0), axis=0)
        return out.astype(q.dtype)

    o = lax.map(block, jnp.arange(n_blocks, dtype=jnp.int32))
    o = jnp.transpose(o, (1, 0, 2, 3, 4))
    return o.reshape(B, S, HEADS_PER_GROUP * HEAD_DIM)

def second_inputs(seed: int = 0) -> dict:
    key = jax.random.key(seed)
    ks = jax.random.split(key, 12)
    f32 = jnp.float32
    x = jax.random.normal(ks[0], (BATCH, SEQ, D_MODEL), f32)
    norm_gain = 1.0 + 0.05 * jax.random.normal(ks[1], (DEPTH_2, D_MODEL), f32)
    w_in = jax.random.normal(ks[2], (DEPTH_2, D_MODEL, IN_W), f32) * D_MODEL ** -0.5
    b_gate = 0.01 * jax.random.normal(ks[3], (DEPTH_2, 2, D_MODEL), f32)
    rel_bias = 0.5 * jax.random.normal(ks[4], (NUM_BUCKETS, N_ATT_HEADS), f32)
    w_pool = jax.random.normal(ks[5], (DEPTH_2, N_POOL_GROUPS, POOL_GROUP_W, POOL_GROUP_W), f32) * POOL_GROUP_W ** -0.5
    pool_scale = 1.0 + 0.1 * jax.random.normal(ks[6], (DEPTH_2, BRANCH_W), f32)
    w_proj_a = jax.random.normal(ks[7], (DEPTH_2, BRANCH_W, D_MODEL), f32) * BRANCH_W ** -0.5
    w_proj_b = jax.random.normal(ks[8], (DEPTH_2, BRANCH_W, D_MODEL), f32) * BRANCH_W ** -0.5
    w_out = jax.random.normal(ks[9], (DEPTH_2, D_MODEL, D_MODEL), f32) * D_MODEL ** -0.5
    final_gain = 1.0 + 0.05 * jax.random.normal(ks[10], (D_MODEL,), f32)
    return {"x": x, "norm_gain": norm_gain, "w_in": w_in, "b_gate": b_gate,
            "rel_bias": rel_bias, "w_pool": w_pool, "pool_scale": pool_scale,
            "w_proj_a": w_proj_a, "w_proj_b": w_proj_b, "w_out": w_out,
            "final_gain": final_gain}

def second_block(x, norm_gain, w_in, b_gate, rel_bias, w_pool, pool_scale,
              w_proj_a, w_proj_b, w_out, final_gain):
    B, S, D = x.shape
    splits = np.cumsum([BRANCH_W, BRANCH_W, QKV_W, QKV_W, QKV_W, BRANCH_W]).tolist()
    for l in range(DEPTH_2):
        h = _rmsnorm(x, norm_gain[l])
        z = h @ w_in[l]
        a_in, a_gate, q, k, v, b_gp, g_logits = jnp.split(z, splits, axis=-1)
        y_a = (_multiscale_pool(a_in, w_pool[l], pool_scale[l]) * jax.nn.silu(a_gate)) @ w_proj_a[l]
        shp = (B, S, N_ATT_GROUPS, HEADS_PER_GROUP, HEAD_DIM)
        att = _dilated_attention(q.reshape(shp), k.reshape(shp), v.reshape(shp), rel_bias)
        y_b = (att * jax.nn.silu(b_gp)) @ w_proj_b[l]
        gates = jax.nn.sigmoid(g_logits.reshape(B, S, 2, D) + b_gate[l])
        merged = gates[:, :, 0] * y_a + gates[:, :, 1] * y_b
        x = x + merged @ w_out[l]
    return _rmsnorm(x, final_gain)


def setup_inputs(seed=0):
    out = dict(first_inputs(seed))
    for name, value in second_inputs(seed + 1).items():
        if name != "x":
            out[name + "_2"] = value
    return out


def reference(
    x, p, positions, g_ffn1, g_mix, g_ffn2, g_ple, ffn1_w_in, ffn1_w_out, ffn2_w_in, ffn2_w_out,
    ple_w_proj, ple_w_gate, mla_w_in, mla_g_q_lat, mla_w_uq, mla_g_kv_lat, mla_w_ukv, mla_g_qn,
    mla_g_kn, mla_w_o, fox_w_in, fox_b_f, fox_g_qn, fox_g_kn, fox_w_o, norm_gain_2, w_in_2,
    b_gate_2, rel_bias_2, w_pool_2, pool_scale_2, w_proj_a_2, w_proj_b_2, w_out_2, final_gain_2,
):
    x = first_block(
        x, p, positions, g_ffn1, g_mix, g_ffn2, g_ple, ffn1_w_in, ffn1_w_out, ffn2_w_in,
        ffn2_w_out, ple_w_proj, ple_w_gate, mla_w_in, mla_g_q_lat, mla_w_uq, mla_g_kv_lat,
        mla_w_ukv, mla_g_qn, mla_g_kn, mla_w_o, fox_w_in, fox_b_f, fox_g_qn, fox_g_kn, fox_w_o,
    )
    return second_block(
        x, norm_gain_2, w_in_2, b_gate_2, rel_bias_2, w_pool_2, pool_scale_2, w_proj_a_2,
        w_proj_b_2, w_out_2, final_gain_2,
    )


_drawn_inputs = setup_inputs


def setup_inputs(seed=0):
    import zlib

    import numpy as np

    out = dict(_drawn_inputs(seed))
    spreads = {}
    factors = {'mla_g_q_lat': 3.292,
     'mla_g_qn': 3.404,
     'mla_g_kn': 3.43,
     'fox_g_qn': 3.068,
     'fox_g_kn': 2.706,
     'norm_gain_2': 3.971,
     'b_gate_2': 28.701,
     'rel_bias_2': 4.641,
     'pool_scale_2': 3.137}
    for name, (base, spread) in spreads.items():
        noise = np.random.default_rng([zlib.crc32(name.encode()), seed]).standard_normal(out[name].shape)
        drawn = base * np.exp(spread * noise) if base else spread * noise
        out[name] = __import__('jax').numpy.asarray(drawn.astype(out[name].dtype))
    for name, factor in factors.items():
        out[name] = (out[name] * factor).astype(out[name].dtype)
    return out
```

```python
from contextlib import ExitStack

import numpy as np
import concourse.bass as bass
from concourse import mybir

F32 = mybir.dt.float32
F32R = mybir.dt.float32r
BF16 = mybir.dt.bfloat16
I32 = mybir.dt.int32
ALU = mybir.AluOpType
ACT = mybir.ActivationFunctionType
AX = mybir.AxisListType.X

P = 128
S = 256
NT = S // P
D = 1024
DK = D // P
FF = 2816
FCH = FF // 256
PLE = 256
H = 16
QR, KVR, ROPE, NOPE = 512, 256, 32, 64
DQ = NOPE + ROPE
LAT = QR + KVR + ROPE
HD = 64
DF = HD + 2
G3, H8 = 3, 8
NH2 = G3 * H8
WIN = 3 * P
EPS = 1e-6
RING = 4
GC = 2048
NEG = -1.0e30
DILATED = ((128, 1), (512, 4), (2048, 16))
POOL_WINDOWS = (2, 4, 8, 16)

G_LAYER, G_QLAT, G_KVLAT, G_NORM2, G_POOL = 32, 64, 68, 70, 78
NORM_GAIN = [0, 8, 16, 24, 32, 40, 48, 56, G_NORM2]

B2_CHUNKS = [("q", 0), ("k", 0), ("v", 0), ("q", 1), ("k", 1), ("v", 1), ("a_in", 0), ("a_gate", 0),
             ("q", 2), ("k", 2), ("v", 2), ("b_gp", 0), ("g", 0), ("g", 1), ("g", 2), ("g", 3)]
B2_COL = {"a_in": 0, "a_gate": 512, "q": 1024, "k": 2560, "v": 4096, "b_gp": 5632, "g": 6144}
B2_FILL = [0, 1, 2, 3, 4, 5, 6, 7, 8, 10, 12, 13, 14, 15, 16, 17]
B2_POOL, B2_MIX, B2_YAT, B2_PA, B2_PERM, B2_YBT, B2_PB, B2_MT, B2_OUT = 9, 11, 18, 19, 21, 22, 23, 25, 27
B2_QKV = [(0, 1, 2), (3, 4, 5), (8, 9, 10)]
B2_HEAD0 = 6


def plan():
    sizes = {
        "norm": (0, 0, (1, 1, 1, 1), (1, 1, 1, 1)),
        "setup": (0, 0, (1, 1, 1, 0), (1, 1, 1, 0)),
        "ffn": (33, 13, (6, 5, 0, 0), (6, 5, 0, 0)),
        "ffn_p": (33, 13, (6, 5, 1, 0), (6, 5, 1, 0)),
        "mla": (13, 11, (H + 2, H + 2, H + 2, H + 1), (2 * H + 2, H + 2, H + 2, H + 1)),
        "fox": (17, 9, (H + 1, H + 1, H + 1, H + 2), (2 * H + 1, H + 1, H + 1, H + 2)),
        "ple": (5, 4, (0, 0, 0, 0), (0, 0, 0, 0)),
        "b2": (40, 29, (NH2,) * 4, (2 * NH2, NH2, NH2, NH2)),
    }
    order = [("n0", "norm"), ("f0", "ffn"), ("setup", "setup"), ("n1", "norm"), ("mla", "mla"), ("n2", "norm"),
             ("f1", "ffn_p"), ("n3", "norm"), ("p0", "ple"), ("n4", "norm"), ("f2", "ffn"), ("n5", "norm"),
             ("fox", "fox"), ("n6", "norm"), ("f3", "ffn_p"), ("n7", "norm"), ("p1", "ple"), ("n8", "norm"),
             ("b2", "b2")]
    g = q = 0
    f, r = [0] * 4, [0] * 4
    at = {}
    for name, kind in order:
        at[name] = (g, q, tuple(f), tuple(r))
        dg, dq, df, dr = sizes[kind]
        g, q = g + dg, q + dq
        f = [a + b for a, b in zip(f, df)]
        r = [a + b for a, b in zip(r, dr)]
    return at, g


PLAN, NGROUPS = plan()


def heads_at():
    before = {"mla": (1, 1, 1, 0), "fox": (0, 0, 0, 1), "b2": (0, 0, 0, 0)}
    return {n: tuple([a + b for a, b in zip(PLAN[n][x], before[n])] for x in (2, 3)) for n in before}


HEADS = heads_at()


def build(nc, I, out):
    with ExitStack() as ctx:
        def sem(name):
            return ctx.enter_context(nc.semaphore(name))

        top = [0]

        def sb(name, shape, dt=F32):
            n = int(np.prod(shape[1:])) * (2 if dt == BF16 else 4)
            t = nc.alloc_sbuf_tensor_at(name, list(shape), dt, offset=BASE + top[0])
            top[0] += (n + 31) // 32 * 32
            return t

        BASE = (nc.sbuf_base + 63) // 64 * 64
        raw = sb("raw", [P, RING, GC])
        wh = sb("wh", [P, RING, GC], F32R)
        wl = sb("wl", [P, RING, GC], F32R)
        h = sb("h", [P, NT, D])
        hn = sb("hn", [P, NT, D])
        xh = sb("xh", [P, DK, S], F32R)
        xl = sb("xl", [P, DK, S], F32R)
        ident = sb("ident", [P, P])
        flip = sb("flip", [P, P])
        tri = sb("tri", [P, P])
        ones = sb("ones", [P, P])
        identb = sb("identb", [P, P], BF16)
        causal = sb("causal", [P, P], BF16)
        gains = sb("gains", [P, 82])
        headg = sb("headg", [P, 4])
        tab = sb("tab", [P, 2, NT, 4, 16])
        ssq = sb("ssq", [P, NT])
        rstd = sb("rstd", [P, NT])
        mhalf = sb("mhalf", [P, 32])
        lss = sb("lss", [P, 2, NT])
        lrs = sb("lrs", [P, 2, NT])
        kss = sb("kss", [P, NT])
        hss = sb("hss", [P, 4, H])
        hrs = sb("hrs", [P, 4, H])
        nmx = sb("nmx", [P, NT, NH2])
        rs = sb("rs", [P, NT, NH2])
        rin = sb("rin", [P, NT, NH2])
        bf = sb("bf", [P, H])
        mxp = sb("mxp", [P, NT])
        fl = sb("fl", [P, 3, NT, H])
        XB = BASE + top[0]

        def region():
            at = [0]

            def x(name, shape, dt=F32, offset=None):
                n = int(np.prod(shape[1:])) * (2 if dt == BF16 else 4)
                o = at[0] if offset is None else offset
                at[0] = max(at[0], o + (n + 31) // 32 * 32)
                return nc.alloc_sbuf_tensor_at(name, list(shape), dt, offset=XB + o)
            return x

        x = region()
        ah = x("ah", [P, 2 * FCH, S], F32R)
        al = x("al", [P, 2 * FCH, S], F32R)
        sg = x("sg", [P, 2, NT, 256])
        a_n = x("a_n", [P, 2, NT, 256])
        p_n = x("p_n", [P, NT, PLE])
        ph = x("ph", [P, 2, S], F32R)
        pl = x("pl", [P, 2, S], F32R)
        pp = x("pp", [P, NT, D])
        x = region()
        gate = x("gate", [P, NT, D])
        x = region()
        qn = x("qn", [P, NT, H * DQ])
        kn = x("kn", [P, NT, H * DQ])
        vn = x("vn", [P, NT, H * HD])
        lat = x("lat", [P, NT, QR + KVR])
        o_l = NT * (H * DQ * 2 + H * HD + QR + KVR) * 4
        lh = x("lh", [P, 6, S], F32R)
        ll = x("ll", [P, 6, S], F32R)
        qkT = x("qkT", [P, 2, 2 * S], offset=o_l)
        probs = x("probs", [P, 2, 3 * P])
        pT = x("pT", [P, 2, 3 * P])
        sqb = x("sqb", [P, 2, H * DQ], offset=o_l + 12 * 1024)
        rt = x("rt", [P, 4, H, 16])
        kpe = x("kpe", [P, NT, ROPE])
        kpr = x("kpr", [P, NT, ROPE])
        x = region()
        x("below", [P, 1], offset=2 * (2 * FCH * S * 4) + 2 * (2 * NT * 256 * 4) - 32)
        causal_f = x("causal_f", [P, P])
        onehot = x("onehot", [33, G3 * 512])
        rb = x("rb", [33, NH2])
        tsb = x("tsb", [H8, G3, 512])
        hraw = x("hraw", [HD, 4])
        rgain = x("rgain", [P, 2, ROPE])
        freq = x("freq", [P, 16])
        posi = x("posi", [P, NT], I32)
        posf = x("posf", [P, NT])
        ang = x("ang", [P, NT, 16])
        turns = x("turns", [P, NT, 16])
        rc = x("rc", [P, 2, NT, 16])
        wrap = x("wrap", [P, NT, 16])
        cs = x("cs", [P, 2, NT, 16])
        x = region()
        qkv = x("qkv", [P, 2, 3, NT, 512])
        win = x("win", [P, 2, WIN])
        oraw = x("oraw", [P, NT, NH2 * HD])
        gts = x("gts", [P, NT, 2 * D])
        o_g = (2 * 3 * NT * 512 + 2 * WIN + NT * NH2 * HD) * 4
        bands = x("bands", [P, 2, 4, S], offset=o_g)
        u = x("u", [P, NT, 512], offset=o_g + 8 * 1024)
        plT = x("plT", [P, 4, S], offset=o_g + 12 * 1024)
        bg = x("bg", [P, 2, 512], offset=o_g + 16 * 1024)
        wp = x("wp", [P, 4, P])
        qkT2 = x("qkT2", [HD, 2, 2 * S])
        pr2 = x("pr2", [P, 2 * S])
        pT2 = x("pT2", [P, 2 * S])
        et = x("et", [P, 512])
        x = region()
        orev = x("orev", [P, NT, 512])
        otmp = x("otmp", [P, NT, 512])
        cmb = x("cmb", [P, 4, NT * NH2])
        x("gap", [P, 1], offset=12 * 1024 - 32)
        mg = x("mg", [P, NT, D])
        fg = x("fg", [P, D])
        s_a = hn[:, 0, :].rearrange("p (t n) -> p t n", t=NT)
        s_b = hn[:, 1, :].rearrange("p (t n) -> p t n", t=NT)

        acc_t = ctx.enter_context(nc.psum_tensor("acc", [P, NT, 2, 512], F32))
        M = ctx.enter_context(nc.psum_tensor("misc", [P, 4, 512], F32))
        scratch = nc.dram_tensor("bias_by_offset", (NH2, 512), F32, kind="Internal")

        def acc(q, t):
            return acc_t[:, t, q % 2, :]

        x_in = sem("x_in")
        ident_in = sem("ident_in")
        small_in = sem("small_in")
        ph_done = sem("ph_done")
        oh_done = sem("oh_done")
        p_in = sem("p_in")
        raw_in = [sem(f"raw_in{i}") for i in range(RING)]
        hi_done = sem("hi_done")
        lo_done = sem("lo_done")
        w_used = sem("w_used")
        acc_ready = sem("acc_ready")
        acc_read = [sem(f"acc_read{i}") for i in range(2)]
        m_ready = [sem(f"m_ready{i}") for i in range(4)]
        m_read = [sem(f"m_read{i}") for i in range(4)]
        h_added = sem("h_added")
        sq_done = sem("sq_done")
        rstd_done = sem("rstd_done")
        hn_done = sem("hn_done")
        xh_done = sem("xh_done")
        silu_done = sem("silu_done")
        ah_done = sem("ah_done")
        gate_done = sem("gate_done")
        lat_sq = sem("lat_sq")
        lat_rstd = sem("lat_rstd")
        lh_done = sem("lh_done")
        heads_sq = sem("heads_sq")
        heads_ss = sem("heads_ss")
        heads_rstd = sem("heads_rstd")
        heads_scaled = sem("heads_scaled")
        heads_ready = sem("heads_ready")
        q_rotated = sem("q_rotated")
        max_done = sem("max_done")
        exp_done = sem("exp_done")
        rin_done = sem("rin_done")
        forget_exp = sem("forget_exp")
        forget_in = sem("forget_in")
        const_ready = sem("const_ready")
        table_out = sem("table_out")
        angles = sem("angles")
        sines = sem("sines")
        power = sem("power")
        v_step = sem("v_step")
        s_step = sem("s_step")
        p_step = sem("p_step")
        win_in = [sem(f"win_in{i}") for i in range(2)]
        biased = sem("biased")
        b2_small = sem("b2_small")
        bg_in = [sem(f"bg_in{i}") for i in range(2)]
        bg_used = sem("bg_used")
        inner_exp = sem("inner_exp")
        gate_sum = sem("gate_sum")
        gate_exp = sem("gate_exp")
        combine_in = sem("combine_in")
        combine_exp = sem("combine_exp")
        o_done = sem("o_done")
        mg_done = sem("mg_done")
        fg_in = sem("fg_in")
        y_done = sem("y_done")
        y_out = sem("y_out")

        def acc_reads(q):
            return 2 * (q // 2) + 2

        def tile_ready(eng, q, t, g, i=0, di=0):
            if t == 0 or g is None:
                eng.wait_ge(acc_ready, q + 1 + di * i)
            else:
                eng.wait_ge(w_used, g + 1 + 2 * di * i)

        def columns(g):
            gm, gx = PLAN["mla"][0], PLAN["fox"][0]
            if g in (gm + 2, gm + 3):
                return 4 * (LAT - QR)
            return DK * H if g == gx else GC

        block = ctx.enter_context(nc.Block())

        def copy_kv(eng, fill, t, n):
            src = acc(fill, t).rearrange("p (h d) -> p h d", d=NOPE + HD)
            dk = kn[:, t, :].rearrange("p (h d) -> p h d", d=DQ)[:, 4 * n:4 * n + 4, 0:NOPE]
            dv = vn[:, t, 4 * n * HD:4 * (n + 1) * HD].rearrange("p (h d) -> p h d", d=HD)
            for dst, part in ((dk, src[:, :, 0:NOPE]), (dv, src[:, :, NOPE:])):
                if eng is nc.scalar:
                    c = nc.scalar.activation(dst, part, ACT.Copy)
                else:
                    c = nc.vector.tensor_copy(dst, part)
            c.then_inc(acc_read[fill % 2], 1)

        @block.sync
        def _(sp):
            def room(g, i=0):
                if g >= RING:
                    sp.wait_ge(lo_done, g - RING + 1 + RING * i)

            def fetch(g, parts, i=0):
                room(g, i)
                for dst, src in parts:
                    sp.dma_start(dst, src).then_inc(raw_in[g % RING], 16)

            def tall(g, w, row, col, n=512):
                dst = raw[:, g % RING, 0:4 * n].rearrange("p (k n) -> p k n", k=4)
                src = w[row:row + 512, col:col + n].rearrange("(k p) n -> p k n", p=P)
                fetch(g, [(dst[:, 2 * j:2 * j + 2, :], src[:, 2 * j:2 * j + 2, :]) for j in range(2)])

            def wide(g, w, row, col=0):
                dst = raw[:, g % RING, :].rearrange("p (k n) -> p k n", k=2)
                src = w[row:row + 256, col:col + D].rearrange("(k p) n -> p k n", p=P)
                fetch(g, [(dst[:, j:j + 1, :], src[:, j:j + 1, :]) for j in range(2)])

            def gate_up(g, w, k, c, i=0):
                dst = raw[:, g % RING, :].rearrange("p (k u n) -> p k u n", k=4, u=2)
                fetch(g, [(dst[:, :, j, :], w[512 * k:512 * k + 512, bass.ds(c * 256 + j * FF, 256)]
                           .rearrange("(k p) n -> p k n", p=P)) for j in range(2)], i)

            def ffn(name, w_in, w_out):
                g0 = PLAN[name][0]
                peel = 3 if g0 == 0 else 1
                for c in range(peel):
                    for k in range(2):
                        gate_up(g0 + 2 * c + k, w_in, k, c)
                with sp.Fori(0, (FCH - peel) // 2) as i:
                    for c in range(2):
                        for k in range(2):
                            gate_up(g0 + 2 * (peel + c) + k, w_in, k, i * 2 + peel + c, i)
                for c in range(FCH):
                    wide(g0 + 2 * FCH + c, w_out, 256 * c)

            for t in range(NT):
                sp.dma_start(h[:, t, :], I["x"][0, t * P:(t + 1) * P, :]).then_inc(x_in, 16)
            ffn("f0", I["ffn1_w_in"][0], I["ffn1_w_out"][0])
            g = PLAN["mla"][0]
            for k in range(2):
                tall(g + k, I["mla_w_in"][0], 512 * k, 0)
            for k in range(2):
                tall(g + 2 + k, I["mla_w_in"][0], 512 * k, 512, LAT - QR)
            for c in range(3):
                tall(g + 4 + c, I["mla_w_uq"][0], 0, 512 * c)
            for c in range(2):
                wide(g + 7 + c, I["mla_w_ukv"][0], 0, D * c)
            for k in range(4):
                wide(g + 9 + k, I["mla_w_o"][0], 256 * k)
            ffn("f1", I["ffn2_w_in"][0], I["ffn2_w_out"][0])

            def ple(name, i):
                g = PLAN[name][0]
                wide(g, I["ple_w_proj"][i], 0)
                for k in range(4):
                    wide(g + 1 + k, I["ple_w_gate"][i], 256 * k)

            ple("p0", 0)
            ffn("f2", I["ffn1_w_in"][1], I["ffn1_w_out"][1])
            g = PLAN["fox"][0]
            dst = raw[:, g % RING, 0:DK * H].rearrange("p (k n) -> p k n", k=DK)
            src = I["fox_w_in"][0][:, 3 * D:3 * D + H].rearrange("(k p) n -> p k n", p=P)
            fetch(g, [(dst[:, 4 * j:4 * j + 4, :], src[:, 4 * j:4 * j + 4, :]) for j in range(2)])
            for c in range(6):
                for k in range(2):
                    tall(g + 1 + 2 * c + k, I["fox_w_in"][0], 512 * k, 512 * c)
            for k in range(4):
                wide(g + 13 + k, I["fox_w_o"][0], 256 * k)
            ffn("f3", I["ffn2_w_in"][1], I["ffn2_w_out"][1])
            ple("p1", 1)
            g = PLAN["b2"][0]
            for c, (what, j) in enumerate(B2_CHUNKS):
                for k in range(2):
                    tall(g + 2 * c + k, I["w_in_2"][0], 512 * k, B2_COL[what] + 512 * j)
            for n, (w, ks) in enumerate([("w_proj_a_2", 2), ("w_proj_b_2", 2), ("w_out_2", 4)]):
                for k in range(ks):
                    wide(g + 32 + 2 * n + k, I[w][0], 256 * k)
            for t in range(NT):
                sp.wait_ge(y_done, t + 1)
                sp.dma_start(out[0, t * P:(t + 1) * P, :], hn[:, t, :]).then_inc(y_out, 16)
            sp.wait_ge(y_out, 16 * NT)

        @block.tensor
        def _(pe):
            def wait_group(g, i=0):
                pe.wait_ge(lo_done, g + 1 + RING * i)

            def open_acc(q, i=0):
                if q >= 2:
                    pe.wait_ge(acc_read[q % 2], acc_reads(q - 2) + 2 * i)

            def open_m(b, reads):
                if reads:
                    pe.wait_ge(m_read[b], reads)

            def products(dst, hi, lo, rhs_h, rhs_l, first, last):
                pe.matmul(dst, hi, rhs_h, start=first, stop=False)
                pe.matmul(dst, hi, rhs_l, start=False, stop=False)
                return pe.matmul(dst, lo, rhs_h, start=False, stop=last)

            def tall_group(g, q, ah_, al_, k0, kts, n, first, last):
                s = g % RING
                for k in range(kts):
                    for t in range(NT):
                        mm = products(acc(q, t)[:, 0:n], ah_[:, k0 + k, t * P:(t + 1) * P],
                                      al_[:, k0 + k, t * P:(t + 1) * P],
                                      wh[:, s, k * n:(k + 1) * n], wl[:, s, k * n:(k + 1) * n],
                                      first and k == 0, last and k == kts - 1)
                        if last and t == 0 and k == kts - 1:
                            mm.then_inc(acc_ready, 1)
                mm.then_inc(w_used, 1)

            def wide_group(g, q, ah_, al_, k0, first, last):
                s = g % RING
                for t in range(NT):
                    for k in range(2):
                        xa = ah_[:, k0 + k, t * P:(t + 1) * P]
                        xb = al_[:, k0 + k, t * P:(t + 1) * P]
                        st, en = first and k == 0, last and k == 1
                        for n in range(2):
                            r = slice(k * D + n * 512, k * D + (n + 1) * 512)
                            pe.matmul(acc(q + n, t), xa, wh[:, s, r], start=st, stop=False)
                            pe.matmul(acc(q + n, t), xa, wl[:, s, r], start=False, stop=False)
                        for n in range(2):
                            r = slice(k * D + n * 512, k * D + (n + 1) * 512)
                            mm = pe.matmul(acc(q + n, t), xb, wh[:, s, r], start=False, stop=en)
                            if en and t == 0:
                                mm.then_inc(acc_ready, 1)
                mm.then_inc(w_used, 1)

            def wide_stage(g0, q, ah_, al_, kts, k_first=0, ready=None):
                open_acc(q)
                open_acc(q + 1)
                for j in range(kts // 2):
                    wait_group(g0 + j)
                    if ready:
                        ready(j)
                    wide_group(g0 + j, q, ah_, al_, k_first + 2 * j, j == 0, j == kts // 2 - 1)

            def turn(b, cols, src, rows=P, m=ident):
                return pe.transpose(M[0:rows, b, cols], src, m[:, :])

            def norm(name, r):
                f, rd = PLAN[name][2:]
                for b in range(4):
                    open_m(b, rd[b])
                for t in range(NT):
                    pe.wait_ge(hn_done, NT * r + t + 1)
                    for k in range(DK):
                        o = (k % 2) * S + t * P
                        mm = turn(k // 2, slice(o, o + P), hn[:, t, k * P:(k + 1) * P])
                        if t == NT - 1 and k % 2:
                            mm.then_inc(m_ready[k // 2], 1)

            def x_ready(name, b):
                pe.wait_ge(m_read[b], PLAN[name][3][b] + 1)

            def ffn(name, nname, with_p=None):
                g0, q0, f0, r0 = PLAN[name]
                ar = [r0[0], r0[1]]

                def chunk(c, i=0, turn_last=True):
                    q, g = q0 + c, g0 + 2 * c
                    open_acc(q, i)
                    for k in range(2):
                        wait_group(g + k, i)
                        if c == 0:
                            x_ready(nname, 2 * k)
                            x_ready(nname, 2 * k + 1)
                        tall_group(g + k, q, xh, xl, 4 * k, 4, 512, k == 0, k == 1)
                        if k == 0 and turn_last:
                            turn_products(c - 1, i)

                def turn_products(c, i=0):
                    b, q = c % 2, q0 + c
                    pe.wait_ge(acc_read[q % 2], acc_reads(q) + 2 * i)
                    if r0[b] + c // 2 > 0:
                        pe.wait_ge(m_read[b], r0[b] + c // 2 + i)
                    for t in range(NT):
                        for k in range(2):
                            mm = turn(b, slice(k * S + t * P, k * S + (t + 1) * P),
                                      a_n[:, b, t, k * P:(k + 1) * P])
                    mm.then_inc(m_ready[b], 1)

                peel = 3 if g0 == 0 else 1
                for c in range(peel):
                    chunk(c, turn_last=c > 0)
                with pe.Fori(0, (FCH - peel) // 2) as i:
                    for c in range(2):
                        chunk(peel + c, i)
                q, g = q0 + FCH, g0 + 2 * FCH
                open_acc(q)
                open_acc(q + 1)
                for c in range(FCH):
                    wait_group(g + c)
                    pe.wait_ge(m_read[c % 2], r0[c % 2] + c // 2 + 1)
                    wide_group(g + c, q, ah, al, 2 * c, c == 0, c == FCH - 1)
                    if c == 0:
                        turn_products(FCH - 1)
                        if with_p is not None:
                            open_m(2, r0[2])
                            pe.wait_ge(p_in, 16 * (with_p + 1))
                            for t in range(NT):
                                for k in range(2):
                                    mm = turn(2, slice(k * S + t * P, k * S + (t + 1) * P),
                                              p_n[:, t, k * P:(k + 1) * P])
                            mm.then_inc(m_ready[2], 1)

            def heads(name, nh, dk, q_of, k_of, v_of, qkT_, pr, pT_, ready, after, full=False):
                base = HEADS[name][1]

                def step(i):
                    if i < nh:
                        ready(i)
                        open_m(0, base[0] + 2 * i)
                        for t in range(NT):
                            if full:
                                pe.matmul(M[0:dk, 0, t * P:(t + 1) * P], q_of(i, t), flip[:, :],
                                          start=True, stop=True)
                            else:
                                turn(0, slice(t * P, (t + 1) * P), q_of(i, t), dk)
                        for t in range(NT):
                            mm = turn(0, slice(S + t * P, S + (t + 1) * P), k_of(i, t), dk)
                        mm.then_inc(m_ready[0], 1)
                    if 0 <= i - 1 < nh:
                        j = i - 1
                        pe.wait_ge(m_read[0], base[0] + 2 * j + 2)
                        open_m(1, base[1] + j)
                        s = j % 2
                        qT, kT = qkT_[0:dk, s, 0:S], qkT_[0:dk, s, S:2 * S]
                        if full:
                            for t in range(NT):
                                mm = pe.matmul(M[:, 1, t * S:(t + 1) * S], qT[:, t * P:(t + 1) * P], kT,
                                               start=True, stop=True)
                        else:
                            pe.matmul(M[:, 1, 0:P], qT[:, 0:P], kT[:, 0:P], start=True, stop=False)
                            pe.matmul(M[:, 1, 0:P], identb[:, :], causal[:, :], start=False, stop=True)
                            pe.matmul(M[:, 1, P:2 * P], qT[:, P:S], kT[:, 0:P], start=True, stop=True)
                            pe.matmul(M[:, 1, 2 * P:3 * P], qT[:, P:S], kT[:, P:S], start=True, stop=False)
                            mm = pe.matmul(M[:, 1, 2 * P:3 * P], identb[:, :], causal[:, :],
                                           start=False, stop=True)
                        mm.then_inc(m_ready[1], 1)
                    if 0 <= i - 2 < nh:
                        j = i - 2
                        if full:
                            pe.wait_ge(exp_done, j + 1)
                        else:
                            pe.wait_ge(m_read[1], base[1] + j + 1)
                        open_m(2, base[2] + j)
                        src = pr if full else pr[:, j % 2]
                        for n in range(4 if full else 3):
                            mm = turn(2, slice(n * P, (n + 1) * P), src[:, n * P:(n + 1) * P])
                        mm.then_inc(m_ready[2], 1)
                    if 0 <= i - 3 < nh:
                        j = i - 3
                        pe.wait_ge(m_read[2], base[2] + j + 1)
                        open_m(3, base[3] + j)
                        src = pT_ if full else pT_[:, j % 2]
                        blocks = [[(0, 0), (1, 1)], [(2, 0), (3, 1)]] if full else [[(0, 0)], [(1, 0), (2, 1)]]
                        for t in range(NT):
                            for n, (col, kt) in enumerate(blocks[t]):
                                mm = pe.matmul(M[:, 3, t * HD:(t + 1) * HD], src[:, col * P:(col + 1) * P],
                                               v_of(j, kt), start=n == 0, stop=n == len(blocks[t]) - 1)
                        mm.then_inc(m_ready[3], 1)
                        after(j)
                return step

            def turn_o(name):
                r = HEADS[name][1]
                pe.wait_ge(m_read[3], r[3] + H)
                for b in range(4):
                    open_m(b, r[b] + (2 * H if b == 0 else H))
                    for k in range(2 * b, 2 * b + 2):
                        for t in range(NT):
                            o = (k % 2) * S + t * P
                            mm = turn(b, slice(o, o + P), hn[:, t, k * P:(k + 1) * P])
                    mm.then_inc(m_ready[b], 1)

            def o_ready(name):
                r = HEADS[name][1]
                return lambda j: pe.wait_ge(m_read[j], r[j] + (2 * H if j == 0 else H) + 1)

            pe.wait_ge(ident_in, 16)
            norm("n0", 0)
            ffn("f0", "n0")

            pe.wait_ge(const_ready, 1)
            for j in range(G3):
                open_m(j, PLAN["setup"][3][j])
                pe.matmul(M[0:H8, j, :], rb[:, H8 * j:H8 * j + H8], onehot[:, 512 * j:512 * j + 512],
                          start=True, stop=True).then_inc(m_ready[j], 1)

            norm("n1", 1)
            g, q, f, r = PLAN["mla"]
            for c, n in enumerate((QR, LAT - QR)):
                open_acc(q + c)
                for k in range(2):
                    wait_group(g + 2 * c + k)
                    if c == 0:
                        x_ready("n1", 2 * k)
                        x_ready("n1", 2 * k + 1)
                    tall_group(g + 2 * c + k, q + c, xh, xl, 4 * k, 4, n, k == 0, k == 1)

            def turn_latents(ks, fill):
                pe.wait_ge(acc_read[fill % 2], acc_reads(fill))
                for k in ks:
                    if k % 2 == 0:
                        open_m(k // 2, r[k // 2])
                    for t in range(NT):
                        o = (k % 2) * S + t * P
                        mm = turn(k // 2, slice(o, o + P), lat[:, t, k * P:(k + 1) * P])
                    if k % 2:
                        mm.then_inc(m_ready[k // 2], 1)

            turn_latents(range(4), q)
            for c in range(3):
                open_acc(q + 2 + c)
                wait_group(g + 4 + c)
                if c == 0:
                    pe.wait_ge(m_read[0], r[0] + 1)
                    pe.wait_ge(m_read[1], r[1] + 1)
                tall_group(g + 4 + c, q + 2 + c, lh, ll, 0, 4, 512, True, True)
                if c == 0:
                    turn_latents(range(4, 6), q + 1)
            for c in range(2):
                wide_stage(g + 7 + c, q + 5 + 2 * c, lh, ll, 2, 4,
                           (lambda j: pe.wait_ge(m_read[2], r[2] + 1)) if c == 0 else None)

            def mla_ready(i):
                if i == 0:
                    pe.wait_ge(q_rotated, 2)
                    pe.wait_ge(heads_ready, 2)

            step = heads("mla", H, DQ, lambda i, t: qn[:, t, i * DQ:(i + 1) * DQ],
                         lambda i, t: kn[:, t, i * DQ:(i + 1) * DQ],
                         lambda i, t: vn[:, t, i * HD:(i + 1) * HD], qkT, probs, pT, mla_ready, lambda j: None)
            for i in range(H + 3):
                step(i)
            turn_o("mla")
            wide_stage(g + 9, q + 9, xh, xl, DK, 0, o_ready("mla"))

            norm("n2", 2)
            ffn("f1", "n2", with_p=0)

            def ple(name, nname, r):
                g, q, _, _ = PLAN[name]
                fr = PLAN["f1" if name == "p0" else "f3"][3][2]
                wide_stage(g, q, ph, pl, 2, 0, lambda j: pe.wait_ge(m_read[2], fr + 1))
                norm(nname, r)
                wide_stage(g + 1, q + 2, xh, xl, DK, 0, lambda j: x_ready(nname, j))

            ple("p0", "n3", 3)
            norm("n4", 4)
            ffn("f2", "n4")

            norm("n5", 5)
            g, q, f, r = PLAN["fox"]
            open_acc(q)
            wait_group(g)
            for b in range(4):
                x_ready("n5", b)
            tall_group(g, q, xh, xl, 0, DK, H, True, True)
            for c in range(6):
                open_acc(q + 1 + c)
                for k in range(2):
                    wait_group(g + 1 + 2 * c + k)
                    tall_group(g + 1 + 2 * c + k, q + 1 + c, xh, xl, 4 * k, 4, 512, k == 0, k == 1)
                if c == 0:
                    pe.wait_ge(forget_in, 2)
                    open_m(3, r[3])
                    pe.matmul(M[:, 3, 0:H], tri[:, :], fl[:, 2, 0, :], start=True, stop=True)
                    pe.matmul(M[:, 3, H:2 * H], ones[:, :], fl[:, 2, 0, :], start=True, stop=False)
                    pe.matmul(M[:, 3, H:2 * H], tri[:, :], fl[:, 2, 1, :], start=False,
                              stop=True).then_inc(m_ready[3], 1)

            def fox_ready(i):
                if i == 0:
                    pe.wait_ge(m_read[3], r[3] + 1)
                for c in (0, 2, 4):
                    fill = q + 1 + c + i // 8
                    if i % 8 == 0:
                        pe.wait_ge(acc_read[fill % 2], acc_reads(fill))

            step = heads("fox", H, DF, lambda i, t: qn[:, t, i * DF:(i + 1) * DF],
                         lambda i, t: kn[:, t, i * DF:(i + 1) * DF],
                         lambda i, t: vn[:, t, i * HD:(i + 1) * HD], qkT, probs, pT, fox_ready, lambda j: None)
            for i in range(H + 3):
                step(i)
            turn_o("fox")
            wide_stage(g + 13, q + 7, xh, xl, DK, 0, o_ready("fox"))

            norm("n6", 6)
            ffn("f3", "n6", with_p=1)
            ple("p1", "n7", 7)

            norm("n8", 8)
            g, q, f, r = PLAN["b2"]

            def b2_ready(i):
                if i % H8 == 0:
                    for c in B2_QKV[i // H8]:
                        fill = q + B2_FILL[c]
                        pe.wait_ge(acc_read[fill % 2], acc_reads(fill))

            def qkv_of(n, i, t):
                j = i % H8
                return qkv[:, (i // H8) % 2, n, t, j * HD:(j + 1) * HD]

            step = heads("b2", NH2, HD, lambda i, t: qkv_of(0, i, t), lambda i, t: qkv_of(1, i, t),
                         lambda i, t: qkv_of(2, i, t), qkT2, pr2, pT2, b2_ready, lambda j: None, full=True)
            at = 0
            for c in range(len(B2_CHUNKS)):
                open_acc(q + B2_FILL[c])
                for k in range(2):
                    wait_group(g + 2 * c + k)
                    if c == 0:
                        x_ready("n8", 2 * k)
                        x_ready("n8", 2 * k + 1)
                    tall_group(g + 2 * c + k, q + B2_FILL[c], xh, xl, 4 * k, 4, 512, k == 0, k == 1)
                    if 2 * c + k >= B2_HEAD0:
                        step(at)
                        at += 1
                if c == 8:
                    fill = q + B2_POOL
                    open_acc(fill)
                    pe.wait_ge(acc_read[(q + B2_FILL[6]) % 2], acc_reads(q + B2_FILL[6]))
                    pe.wait_ge(b2_small, 16 * 2)
                    for j in range(4):
                        for t in range(NT):
                            mm = pe.matmul(acc(fill, j // 2)[:, (j % 2) * S:(j % 2 + 1) * S],
                                           u[:, t, j * P:(j + 1) * P], bands[:, t, j, :],
                                           start=t == 0, stop=t == NT - 1)
                    mm.then_inc(acc_ready, 1)
                if c == 9:
                    fill = q + B2_MIX
                    open_acc(fill)
                    pe.wait_ge(acc_read[(q + B2_POOL) % 2], acc_reads(q + B2_POOL))
                    for t in range(NT):
                        for j in range(4):
                            mm = pe.matmul(acc(fill, t)[:, j * P:(j + 1) * P], plT[:, j, t * P:(t + 1) * P],
                                           wp[:, j, :], start=True, stop=True)
                    mm.then_inc(acc_ready, 1)

            def turn_fill(fill, rows, ks=4):
                open_acc(fill)
                for k in range(ks):
                    for t in range(NT):
                        o = (k % 2) * S + t * P
                        mm = pe.transpose(acc(fill, k // 2)[:, o:o + P], rows[:, t, k * P:(k + 1) * P],
                                          ident[:, :])
                mm.then_inc(acc_ready, 1)

            pe.wait_ge(acc_read[(q + B2_MIX) % 2], acc_reads(q + B2_MIX))
            turn_fill(q + B2_YAT, s_a)
            step(at)
            wide_stage(g + 32, q + B2_PA, xh, xl, 4, 0,
                       lambda j: pe.wait_ge(acc_read[(q + B2_YAT) % 2], acc_reads(q + B2_YAT)) if j == 0 else None)
            fill = q + B2_PERM
            open_acc(fill)
            pe.wait_ge(o_done, 1)
            for t in range(NT):
                mm = pe.matmul(acc(fill, t), flip[:, :], orev[:, t, :], start=True, stop=True)
            mm.then_inc(acc_ready, 1)
            pe.wait_ge(acc_read[fill % 2], acc_reads(fill))
            turn_fill(q + B2_YBT, otmp)
            wide_stage(g + 34, q + B2_PB, xh, xl, 4, 4,
                       lambda j: pe.wait_ge(acc_read[(q + B2_YBT) % 2], acc_reads(q + B2_YBT)) if j == 0 else None)
            pe.wait_ge(mg_done, 1)
            for j in range(2):
                turn_fill(q + B2_MT + j, mg[:, :, 512 * j:512 * j + 512])
            wide_stage(g + 36, q + B2_OUT, xh, xl, DK, 0,
                       lambda j: pe.wait_ge(acc_read[(q + B2_MT + j // 2) % 2], acc_reads(q + B2_MT + j // 2))
                       if j % 2 == 0 else None)

        def rows_ready(eng, r, t):
            if r == 0:
                eng.wait_ge(x_in, 16 * NT)
            elif r in (4, 8):
                eng.wait_ge(h_added, NT * (r // 4 - 1) + t + 1)
            else:
                q = {1: PLAN["f0"][1] + 12, 2: PLAN["mla"][1] + 10, 3: PLAN["f1"][1] + 12,
                     5: PLAN["f2"][1] + 12, 6: PLAN["fox"][1] + 8, 7: PLAN["f3"][1] + 12,
                     9: PLAN["b2"][1] + B2_OUT + 1}[r]
                eng.wait_ge(acc_read[q % 2], acc_reads(q) - 1 + t)

        SMALL = 9
        FIRST_SILU = {"f0": 0, "f1": 1, "f2": 2, "f3": 3}
        OH = {"mla": 0, "fox": 4, "b2": 8}

        @block.scalar
        def _(act):
            act.dma_start(ident[:, :], I["c_mats"][0]).then_inc(ident_in, 16)
            act.dma_start(gains[:, :], I["gains"]).then_inc(small_in, 16)
            act.dma_start(flip[:, :], I["c_mats"][1]).then_inc(small_in, 16)
            act.dma_start(tri[:, :], I["c_mats"][2]).then_inc(small_in, 16)
            act.dma_start(causal_f[:, :], I["c_mats"][3]).then_inc(small_in, 16)
            act.dma_start(onehot[:, :], I["c_onehot"]).then_inc(small_in, 16)
            act.dma_start(rb[0:32, :], I["rel_bias_2"]).then_inc(small_in, 16)
            act.dma_start(hraw[:, :], I["head_gains"]).then_inc(small_in, 16)
            act.dma_start(rgain[:, :, :], bass.AP(I["rope_gains"].tensor, 0, [[0, P], [ROPE, 2], [1, ROPE]]))\
               .then_inc(small_in, 16)
            act.dma_start(bf[:, :], bass.AP(I["fox_b_f"].tensor, 0, [[0, P], [1, H]])).then_inc(small_in, 16)
            act.dma_start(freq[:, :], bass.AP(I["c_freq"].tensor, 0, [[0, P], [1, 16]])).then_inc(angles, 16)
            act.dma_start(posi[:, :], I["pos"]).then_inc(angles, 16)

            done = [0]

            def split(g, i=0):
                s, n = g % RING, columns(g)
                act.wait_ge(raw_in[s], 32 * (g // RING + 1) + 32 * i)
                if g >= RING:
                    act.wait_ge(w_used, g - RING + 1 + RING * i)
                act.activation(wh[:, s, 0:n], raw[:, s, 0:n], ACT.Copy).then_inc(hi_done, 1)

            def split_to(n):
                for g in range(done[0], min(n, NGROUPS)):
                    split(g)
                done[0] = max(done[0], min(n, NGROUPS))

            def squares(r):
                for t in range(NT):
                    rows_ready(act, r, t)
                    act.activation(hn[:, t, :], h[:, t, :], ACT.Square, accum_out=ssq[:, t:t + 1])\
                       .then_inc(sq_done, 1)

            def round_x(name, r):
                f = PLAN[name][2]
                for k in range(DK):
                    act.wait_ge(m_ready[k // 2], f[k // 2] + 1)
                    c = NORM_GAIN[r] + k
                    act.activation(xh[:, k, :], M[:, k // 2, (k % 2) * S:(k % 2 + 1) * S], ACT.Copy,
                                   scale=gains[:, c:c + 1]).then_inc(xh_done, 1)

            def ffn(name, first=False):
                g0, q0, f0, _ = PLAN[name]

                def silus(c, i=0):
                    q, g = q0 + c, g0 + 2 * c + 1
                    for t in range(NT):
                        tile_ready(act, q, t, g, i, 2)
                        act.activation(sg[:, c % 2, t, :], acc(q, t)[:, 0:256], ACT.Silu).then_inc(silu_done, 1)

                def round_a(c, i=0):
                    b = c % 2
                    act.wait_ge(m_ready[b], f0[b] + c // 2 + 1 + i)
                    act.activation(ah[:, bass.ds(i * 4 + 2 * c, 2), :],
                                   M[:, b, :].rearrange("p (k n) -> p k n", k=2), ACT.Copy).then_inc(ah_done, 1)

                peel = 3 if g0 == 0 else 1
                for c in range(peel):
                    split_to(g0 + 2 * c + 3)
                    if c:
                        round_a(c - 1)
                    split_to(g0 + 2 * c + 4)
                    silus(c)
                with act.Fori(0, (FCH - peel) // 2) as i:
                    for c in range(peel, peel + 2):
                        split(g0 + 2 * c + 2, i)
                        round_a(c - 1, i)
                        split(g0 + 2 * c + 3, i)
                        silus(c, i)
                done[0] = g0 + 2 * FCH + 2
                split_to(g0 + 2 * FCH + 3)
                round_a(FCH - 1)
                if name in ("f1", "f3"):
                    act.wait_ge(m_ready[2], f0[2] + 1)
                    act.activation(ph[:, :, :], M[:, 2, :].rearrange("p (k n) -> p k n", k=2), ACT.Copy)\
                       .then_inc(ph_done, 1)
                split_to(g0 + 3 * FCH + 2)

            squares(0)
            split_to(2)
            act.wait_ge(small_in, 16 * SMALL)
            round_x("n0", 0)
            act.wait_ge(angles, 16 * 2 + 1)
            act.activation(cs[:, :, :, :], rc[:, :, :, :], ACT.Sin).then_inc(sines, 1)
            ffn("f0")
            act.wait_ge(m_read[2], PLAN["setup"][3][2] + 1)
            act.dma_start(scratch[:, :].rearrange("(g h) n -> h g n", g=G3), tsb[:, :, :]).then_inc(table_out, 16)

            squares(1)
            round_x("n1", 1)
            act.wait_ge(table_out, 16)
            g, q, f, r = PLAN["mla"]
            split_to(g + 1 + 3)
            for t in range(NT):
                tile_ready(act, q, t, g + 1)
                act.activation(lat[:, t, 0:QR], acc(q, t)[:, 0:QR], ACT.Square, accum_out=lss[:, 0, t:t + 1])\
                   .then_inc(lat_sq, 1)
            split_to(g + 3 + 3)
            for t in range(NT):
                tile_ready(act, q + 1, t, g + 3)
                act.activation(lat[:, t, QR:QR + KVR], acc(q + 1, t)[:, 0:KVR], ACT.Square,
                               accum_out=lss[:, 1, t:t + 1]).then_inc(lat_sq, 1)
                act.activation(rt[:, t, 0:2, :], acc(q + 1, t)[:, KVR:KVR + ROPE].rearrange("p (a b) -> p a b", a=2), ACT.Square,
                               accum_out=kss[:, t:t + 1]).then_inc(lat_sq, 1)

            def round_latents(ks):
                for k in ks:
                    act.wait_ge(m_ready[k // 2], f[k // 2] + 1)
                    c = G_QLAT + k
                    act.activation(lh[:, k, :], M[:, k // 2, (k % 2) * S:(k % 2 + 1) * S], ACT.Copy,
                                   scale=gains[:, c:c + 1]).then_inc(lh_done, 1)

            round_latents(range(4))
            for c in range(3):
                split_to(g + 4 + c + 3)
                if c == 1:
                    round_latents(range(4, 6))
                for t in range(NT):
                    tile_ready(act, q + 2 + c, t, g + 4 + c)
                    act.activation(qn[:, t, 512 * c:512 * c + 512], acc(q + 2 + c, t), ACT.Copy)\
                       .then_inc(acc_read[(q + 2 + c) % 2], 1)
            split_to(g + 10)
            for t in range(NT):
                for fill in (q + 3, q + 4):
                    act.wait_ge(acc_read[fill % 2], acc_reads(fill))
                act.activation(sqb[:, t, :], qn[:, t, :], ACT.Square).then_inc(heads_sq, 1)
            for c in range(2):
                for n in range(2):
                    fill = q + 5 + 2 * c + n
                    tile_ready(act, fill, 0, g + 7 + c)
                    copy_kv(nc.scalar, fill, 0, 2 * c + n)
                split_to(g + 7 + c + 4)
            for t in range(NT):
                for n in range(4):
                    fill = q + 5 + n
                    act.wait_ge(acc_read[fill % 2], acc_reads(fill) - 1 + t)
                act.wait_ge(acc_read[(q + 8) % 2], acc_reads(q + 8))
                act.wait_ge(acc_read[(q + 7) % 2], acc_reads(q + 7))
                act.wait_ge(heads_ss, t + 1)
                act.activation(sqb[:, t, 0:H * NOPE].rearrange("p (h d) -> p h d", d=NOPE),
                               kn[:, t, :].rearrange("p (h d) -> p h d", d=DQ)[:, :, 0:NOPE],
                               ACT.Square).then_inc(heads_sq, 1)
            split_to(g + 13)

            def heads(name, nh, dk, col):
                f, _ = HEADS[name]
                first = 0 if name == "mla" else H

                def step(i):
                    if i < nh:
                        act.wait_ge(m_ready[0], f[0] + i + 1)
                        if i >= 2:
                            act.wait_ge(m_ready[1], f[1] + i - 1)
                        act.activation(qkT[0:dk, i % 2, 0:S], M[0:dk, 0, 0:S], ACT.Copy,
                                       scale=headg[0:dk, col:col + 1]).then_inc(m_read[0], 1)
                    j = i - 1
                    if 0 <= j < nh:
                        act.wait_ge(max_done, first + j + 1)
                        if j >= 2:
                            act.wait_ge(m_ready[2], f[2] + j - 1)
                        for t, (a, b) in enumerate(((0, P), (P, 3 * P))):
                            e = act.activation(probs[:, j % 2, a:b], M[:, 1, a:b], ACT.Exp,
                                               bias=nmx[:, t, j:j + 1], accum_out=rs[:, t, j:j + 1])
                        e.then_inc(m_read[1], 1)
                return step

            def round_o(name):
                f, _ = HEADS[name]
                for b in range(4):
                    act.wait_ge(m_ready[b], f[b] + H + 1)
                    act.activation(xh[:, 2 * b:2 * b + 2, :], M[:, b, :].rearrange("p (k n) -> p k n", k=2),
                                   ACT.Copy).then_inc(oh_done, 1)

            step = heads("mla", H, DQ, 0)
            for i in range(H + 1):
                step(i)
            round_o("mla")
            split_to(g + 12 + 3)
            squares(2)
            round_x("n2", 2)
            ffn("f1")

            def ple(name, nname, r):
                g, q, _, _ = PLAN[name]
                squares(r)
                for t in range(NT):
                    for n in range(2):
                        tile_ready(act, q + n, t, g)
                        act.activation(pp[:, t, 512 * n:512 * n + 512], acc(q + n, t), ACT.Copy)\
                           .then_inc(acc_read[(q + n) % 2], 1)
                split_to(g + 1 + 3)
                round_x(nname, r)
                split_to(g + 4 + 3)
                for t in range(NT):
                    for n in range(2):
                        fill = q + 2 + n
                        tile_ready(act, fill, t, g + 4)
                        act.activation(gate[:, t, 512 * n:512 * n + 512], acc(fill, t), ACT.Sigmoid)\
                           .then_inc(acc_read[fill % 2], 1)

            ple("p0", "n3", 3)
            squares(4)
            round_x("n4", 4)
            ffn("f2")

            squares(5)
            round_x("n5", 5)
            g, q, f, r = PLAN["fox"]
            split_to(g + 3)
            act.wait_ge(acc_read[q % 2], acc_reads(q))
            act.activation(fl[:, 1, :, :], fl[:, 0, :, :], ACT.Abs).then_inc(forget_exp, 1)
            act.wait_ge(forget_exp, 1)
            act.activation(fl[:, 1, :, :], fl[:, 1, :, :], ACT.Exp, scale=-1.0).then_inc(forget_exp, 1)
            act.wait_ge(forget_exp, 2)
            act.activation(fl[:, 1, :, :], fl[:, 1, :, :], ACT.Ln, bias=1.0).then_inc(forget_exp, 1)
            for c in range(6):
                e = g + 2 + 2 * c
                split_to(e + 3)
                for t in range(NT):
                    fill = q + 1 + c
                    tile_ready(act, fill, t, e)
                    if c < 4:
                        n = 4 + 2 * c + t
                        if n >= 6:
                            act.wait_ge(heads_ss, n - 1)
                        act.activation(sqb[:, t, 0:512], acc(fill, t), ACT.Square).then_inc(heads_sq, 1)
                    else:
                        act.activation(vn[:, t, 512 * (c - 4):512 * (c - 3)], acc(fill, t), ACT.Copy)\
                           .then_inc(acc_read[fill % 2], 1)
            split_to(g + 17)
            step = heads("fox", H, DF, 2)
            for i in range(H + 1):
                step(i)
            round_o("fox")
            split_to(g + 16 + 3)
            squares(6)
            round_x("n6", 6)
            ffn("f3")
            ple("p1", "n7", 7)

            squares(8)
            round_x("n8", 8)
            g, q, f, r = PLAN["b2"]
            hf = HEADS["b2"][0]

            def b2_step(i):
                if i < NH2:
                    act.wait_ge(m_ready[0], hf[0] + i + 1)
                    if i >= 2:
                        act.wait_ge(m_ready[1], hf[1] + i - 1)
                    act.activation(qkT2[:, i % 2, 0:S], M[0:HD, 0, 0:S], ACT.Copy, scale=HD ** -0.5)\
                       .then_inc(m_read[0], 1)
                j = i - 1
                if 0 <= j < NH2:
                    act.wait_ge(max_done, 2 * H + j + 1)
                    for t in range(NT):
                        e = act.activation(pr2[:, t * S:(t + 1) * S], pr2[:, t * S:(t + 1) * S], ACT.Exp,
                                           bias=nmx[:, t, j:j + 1], accum_out=rs[:, t, j:j + 1])
                    e.then_inc(exp_done, 1)

            inner = 0
            at = 0
            for c, (what, j) in enumerate(B2_CHUNKS):
                fill = q + B2_FILL[c]
                for k in range(2):
                    w = 2 * c + k
                    split_to(g + w + 3)
                    if k == 1:
                        for t in range(NT):
                            if what in ("q", "v"):
                                tile_ready(act, fill, t, g + w)
                                act.activation(qkv[:, j % 2, 0 if what == "q" else 2, t, :], acc(fill, t),
                                               ACT.Copy).then_inc(acc_read[fill % 2], 1)
                            elif what in ("a_gate", "b_gp"):
                                tile_ready(act, fill, t, g + w)
                                if inner:
                                    act.wait_ge(gate_sum, inner)
                                act.activation(et[:, :], acc(fill, t), ACT.Exp, scale=-1.0)\
                                   .then_inc(inner_exp, 1)
                                inner += 1
                            elif what == "g":
                                act.wait_ge(acc_read[fill % 2], acc_reads(fill) - 1 + t)
                                part = gts[:, t, 512 * j:512 * j + 512]
                                act.activation(part, part, ACT.Exp, scale=-1.0).then_inc(gate_exp, 1)
                    if w >= B2_HEAD0:
                        b2_step(at)
                        at += 1
                if c == 8:
                    pf = q + B2_POOL
                    for t in range(NT):
                        tile_ready(act, pf, t, None)
                        act.activation(plT[:, 2 * t:2 * t + 2, :],
                                       acc(pf, t).rearrange("p (k n) -> p k n", k=2), ACT.Copy)\
                           .then_inc(acc_read[pf % 2], 1)
            assert at == NH2 + 2

            pf = q + B2_YAT
            for k in range(4):
                act.wait_ge(acc_ready, pf + 1)
                act.activation(xh[:, k, :], acc(pf, k // 2)[:, (k % 2) * S:(k % 2 + 1) * S], ACT.Copy,
                               scale=gains[:, G_POOL + k:G_POOL + k + 1]).then_inc(oh_done, 1)
            act.wait_ge(combine_in, 1)
            act.activation(cmb[:, 2, :], cmb[:, 1, :], ACT.Exp).then_inc(combine_exp, 1)
            split_to(g + 36)
            pf = q + B2_YBT
            for b in range(2):
                act.wait_ge(acc_ready, pf + 1)
                act.activation(xh[:, 4 + 2 * b:6 + 2 * b, :], acc(pf, b).rearrange("p (k n) -> p k n", k=2),
                               ACT.Copy).then_inc(oh_done, 1)
            split_to(g + 38)
            for n in range(4):
                pf = q + B2_MT + n // 2
                act.wait_ge(acc_ready, pf + 1)
                act.activation(xh[:, 2 * n:2 * n + 2, :], acc(pf, n % 2).rearrange("p (k n) -> p k n", k=2),
                               ACT.Copy).then_inc(oh_done, 1)
            split_to(g + 40)
            squares(9)

        @block.vector
        def _(dve):
            done = [0]
            steps = [0]

            def link(ins):
                steps[0] += 1
                ins.then_inc(v_step, 1)
                dve.wait_ge(v_step, steps[0])

            def split(g, i=0):
                s, n = g % RING, columns(g)
                dve.wait_ge(hi_done, g + 1 + RING * i)
                dve.tensor_tensor(wl[:, s, 0:n], raw[:, s, 0:n], wh[:, s, 0:n].bitcast(F32), ALU.subtract)\
                   .then_inc(lo_done, 1)

            def split_to(n):
                for g in range(done[0], min(n, NGROUPS)):
                    split(g)
                done[0] = max(done[0], min(n, NGROUPS))

            def scale_rows(r):
                for t in range(NT):
                    dve.wait_ge(rstd_done, NT * r + t + 1)
                    dve.tensor_scalar(hn[:, t, :], h[:, t, :], rstd[:, t:t + 1], None, ALU.mult)\
                       .then_inc(hn_done, 1)

            def rest_x(name, r):
                for k in range(DK):
                    if k % 2 == 0:
                        dve.wait_ge(xh_done, DK * r + k + 2)
                    c = NORM_GAIN[r] + k
                    e = dve.scalar_tensor_tensor(xl[:, k, :], M[:, k // 2, (k % 2) * S:(k % 2 + 1) * S],
                                                 gains[:, c:c + 1], xh[:, k, :].bitcast(F32),
                                                 ALU.mult, ALU.subtract)
                    if k % 2:
                        e.then_inc(m_read[k // 2], 1)

            def pair(ap):
                return ap.rearrange("p (k n) -> p k n", k=2)

            def residual(q, g, scale):
                for t in range(NT):
                    for n in range(2):
                        tile_ready(dve, q + n, t, g)
                        part = h[:, t, 512 * n:512 * n + 512]
                        dve.scalar_tensor_tensor(part, acc(q + n, t), scale, part, ALU.mult, ALU.add)\
                           .then_inc(acc_read[(q + n) % 2], 1)

            def ffn(name):
                g0, q0, f0, _ = PLAN[name]
                base = FIRST_SILU[name] * FCH

                def gated(c, i=0):
                    q = q0 + c
                    for t in range(NT):
                        dve.wait_ge(silu_done, NT * (base + c) + t + 1 + 4 * i)
                        dve.tensor_tensor(a_n[:, c % 2, t, :], sg[:, c % 2, t, :], acc(q, t)[:, 256:512],
                                          ALU.mult).then_inc(acc_read[q % 2], 1)

                def rest_a(c, i=0):
                    b = c % 2
                    dve.wait_ge(ah_done, base + c + 1 + 2 * i)
                    dve.tensor_tensor(al[:, bass.ds(i * 4 + 2 * c, 2), :], pair(M[:, b, :]),
                                      ah[:, bass.ds(i * 4 + 2 * c, 2), :].bitcast(F32), ALU.subtract)\
                       .then_inc(m_read[b], 1)

                peel = 3 if g0 == 0 else 1
                for c in range(peel):
                    split_to(g0 + 2 * c + 3)
                    if c:
                        rest_a(c - 1)
                    split_to(g0 + 2 * c + 4)
                    gated(c)
                with dve.Fori(0, (FCH - peel) // 2) as i:
                    for c in range(peel, peel + 2):
                        split(g0 + 2 * c + 2, i)
                        rest_a(c - 1, i)
                        split(g0 + 2 * c + 3, i)
                        gated(c, i)
                done[0] = g0 + 2 * FCH + 2
                split_to(g0 + 2 * FCH + 3)
                rest_a(FCH - 1)
                if name in ("f1", "f3"):
                    dve.wait_ge(ph_done, 1 if name == "f1" else 2)
                    dve.tensor_tensor(pl[:, :, :], pair(M[:, 2, :]), ph[:, :, :].bitcast(F32), ALU.subtract)\
                       .then_inc(m_read[2], 1)
                split_to(g0 + 3 * FCH + 2)
                residual(q0 + FCH, g0 + 3 * FCH - 1, 0.5)

            scale_rows(0)
            split_to(2)
            dve.wait_ge(small_in, 16 * SMALL)
            rest_x("n0", 0)

            dve.memset(ones[:, :], 1.0).then_inc(v_step, 1)
            steps[0] += 1
            dve.wait_ge(angles, 16 * 2)
            link(dve.tensor_copy(posf[:, :], posi[:, :]))
            for t in range(NT):
                link(dve.tensor_scalar(ang[:, t, :], freq[:, :], posf[:, t:t + 1], None, ALU.mult))
            big = 1.5 * 2.0 ** 23
            link(dve.tensor_scalar(turns[:, :, :], ang[:, :, :], 1.0 / (2.0 * np.pi), None, ALU.mult))
            link(dve.tensor_scalar(turns[:, :, :], turns[:, :, :], big, None, ALU.add))
            link(dve.tensor_scalar(turns[:, :, :], turns[:, :, :], -big, None, ALU.add))
            c1 = 6.28125
            c2 = float(np.float32(np.round((2 * np.pi - c1) * 2.0 ** 20) / 2.0 ** 20))
            c3 = float(np.float32(2 * np.pi - c1 - c2))
            for part in (c1, c2, c3):
                link(dve.scalar_tensor_tensor(ang[:, :, :], turns[:, :, :], -part, ang[:, :, :],
                                              ALU.mult, ALU.add))
            link(dve.tensor_scalar(rc[:, 0, :, :], ang[:, :, :], float(np.pi / 2), None, ALU.add))
            link(dve.tensor_scalar(wrap[:, :, :], rc[:, 0, :, :], float(np.pi), -2.0 * float(np.pi),
                                   ALU.is_gt, ALU.mult))
            link(dve.tensor_tensor(rc[:, 0, :, :], rc[:, 0, :, :], wrap[:, :, :], ALU.add))
            lim = float(np.nextafter(np.float32(np.pi), np.float32(0)))
            link(dve.tensor_scalar(rc[:, 0, :, :], rc[:, 0, :, :], lim, -lim, ALU.min, ALU.max))
            dve.tensor_scalar(rc[:, 1, :, :], ang[:, :, :], lim, -lim, ALU.min, ALU.max).then_inc(angles, 1)
            dve.memset(headg[:, 1:4], 1.0).then_inc(v_step, 1)
            link(dve.memset(headg[:, 0:1], DQ ** -0.5))
            steps[0] += 1
            dve.wait_ge(v_step, steps[0])
            for n, scale in enumerate((DQ ** -0.5, 1.0, HD ** -0.5, 1.0)):
                link(dve.tensor_scalar(headg[0:HD, n:n + 1], hraw[:, n:n + 1], scale, None, ALU.mult))
            link(dve.tensor_copy(identb[:, :], ident[:, :]))
            link(dve.tensor_copy(causal[:, :], causal_f[:, :]))
            link(dve.memset(rb[32:33, :], NEG))
            dve.wait_ge(sines, 1)
            for n in range(2):
                for t in range(NT):
                    for c, (half, fn) in enumerate(((0, 0), (1, 1), (0, 1), (1, 0))):
                        link(dve.tensor_tensor(tab[:, n, t, c, :], rgain[:, n, 16 * half:16 * half + 16],
                                               cs[:, fn, t, :], ALU.mult))
            dve.tensor_copy(mxp[:, :], posf[:, :]).then_inc(const_ready, 1)
            ffn("f0")
            f = PLAN["setup"][2]
            for j in range(G3):
                dve.wait_ge(m_ready[j], f[j] + 1)
                dve.tensor_copy(tsb[:, j, :], M[0:H8, j, :]).then_inc(m_read[j], 1)

            scale_rows(1)
            rest_x("n1", 1)
            g, q, f, r = PLAN["mla"]
            split_to(g + 1 + 3)
            for t in range(NT):
                dve.wait_ge(lat_rstd, t + 1)
                dve.tensor_scalar(lat[:, t, 0:QR], acc(q, t), lrs[:, 0, t:t + 1], None, ALU.mult)\
                   .then_inc(acc_read[q % 2], 1)
            split_to(g + 3 + 3)
            for t in range(NT):
                dve.wait_ge(lat_sq, 2 + 2 * t + 2)
                dve.tensor_copy(kpe[:, t, :], acc(q + 1, t)[:, KVR:KVR + ROPE])
                dve.wait_ge(lat_rstd, 2 + t + 1)
                dve.tensor_scalar(lat[:, t, QR:QR + KVR], acc(q + 1, t)[:, 0:KVR], lrs[:, 1, t:t + 1], None,
                                  ALU.mult).then_inc(acc_read[(q + 1) % 2], 1)

            def rest_latents(ks):
                for k in ks:
                    if k % 2 == 0:
                        dve.wait_ge(lh_done, k + 2)
                    c = G_QLAT + k
                    e = dve.scalar_tensor_tensor(ll[:, k, :], M[:, k // 2, (k % 2) * S:(k % 2 + 1) * S],
                                                 gains[:, c:c + 1], lh[:, k, :].bitcast(F32),
                                                 ALU.mult, ALU.subtract)
                    if k % 2:
                        e.then_inc(m_read[k // 2], 1)

            def rotate(eng, x1, x2, table, tmp, ln):
                for n, (x, c) in enumerate(((x1, 0), (x2, 1), (x1, 2), (x2, 3))):
                    ln(eng.tensor_tensor(tmp[n], x, table[c], ALU.mult))
                ln(eng.tensor_tensor(x1, tmp[0], tmp[1], ALU.subtract))
                ln(eng.tensor_tensor(x2, tmp[2], tmp[3], ALU.add))

            rest_latents(range(4))
            dve.wait_ge(acc_read[(q + 1) % 2], acc_reads(q + 1))
            for t in range(NT):
                rotate(dve, kpe[:, t, 0:16], kpe[:, t, 16:32], [tab[:, 1, t, c, :] for c in range(4)],
                       [kpr[:, 0, 0:16], kpr[:, 0, 16:32], kpr[:, 1, 0:16], kpr[:, 1, 16:32]], link)
            for c in range(3):
                split_to(g + 4 + c + 3)
                if c == 1:
                    rest_latents(range(4, 6))
            split_to(g + 10)
            heads3 = lambda ap, d: ap.rearrange("p (h d) -> p h d", d=d)
            for t in range(NT):
                dve.wait_ge(heads_sq, t + 1)
                dve.tensor_reduce(hss[:, t, :], heads3(sqb[:, t, :], DQ), AX, ALU.add).then_inc(heads_ss, 1)
            for c in range(2):
                for n in range(2):
                    fill = q + 5 + 2 * c + n
                    tile_ready(dve, fill, 1, g + 7 + c)
                    copy_kv(nc.vector, fill, 1, 2 * c + n)
                split_to(g + 7 + c + 4)
                t = c
                dve.wait_ge(heads_rstd, t + 1)
                qv = heads3(qn[:, t, :], DQ)
                dve.tensor_tensor(qv, qv, hrs[:, t, :].unsqueeze(2).to_broadcast([P, H, DQ]), ALU.mult)\
                   .then_inc(heads_scaled, 1)
            for t in range(NT):
                dve.wait_ge(heads_sq, NT + t + 1)
                link(dve.tensor_reduce(hss[:, 2 + t, :], heads3(sqb[:, t, 0:H * NOPE], NOPE), AX, ALU.add))
                dve.tensor_scalar(hss[:, 2 + t, :], hss[:, 2 + t, :], kss[:, t:t + 1], None, ALU.add)\
                   .then_inc(heads_ss, 1)
            for t in range(NT):
                dve.wait_ge(heads_rstd, NT + t + 1)
                kv = heads3(kn[:, t, :], DQ)
                dve.tensor_tensor(kv[:, :, 0:NOPE], kv[:, :, 0:NOPE],
                                  hrs[:, 2 + t, :].unsqueeze(2).to_broadcast([P, H, NOPE]), ALU.mult)
                dve.tensor_tensor(kv[:, :, NOPE:DQ], kpe[:, t, :].unsqueeze(1).to_broadcast([P, H, ROPE]),
                                  hrs[:, 2 + t, :].unsqueeze(2).to_broadcast([P, H, ROPE]), ALU.mult)\
                   .then_inc(heads_ready, 1)
            split_to(g + 13)

            def heads(name, nh, dk, col):
                f, r = HEADS[name]

                def step(i):
                    if i < nh:
                        dve.wait_ge(m_ready[0], f[0] + i + 1)
                        if i >= 2:
                            dve.wait_ge(m_ready[1], f[1] + i - 1)
                        dve.wait_ge(m_read[0], r[0] + 2 * i + 1)
                        dve.tensor_scalar(qkT[0:dk, i % 2, S:2 * S], M[0:dk, 0, S:2 * S],
                                          headg[0:dk, col:col + 1], None, ALU.mult).then_inc(m_read[0], 1)
                    j = i - 1
                    if 0 <= j < nh:
                        dve.wait_ge(m_ready[1], f[1] + j + 1)
                        dve.tensor_reduce(nmx[:, 0, j:j + 1], M[:, 1, 0:P], AX, ALU.max, negate=True)
                        dve.tensor_reduce(nmx[:, 1, j:j + 1], M[:, 1, P:3 * P], AX, ALU.max, negate=True)\
                           .then_inc(max_done, 1)
                    j = i - 2
                    if 0 <= j < nh:
                        dve.wait_ge(m_ready[2], f[2] + j + 1)
                        if j >= 2:
                            dve.wait_ge(m_ready[3], f[3] + j - 1)
                        dve.tensor_copy(pT[:, j % 2, :], M[:, 2, 0:3 * P]).then_inc(m_read[2], 1)
                        dve.wait_ge(m_read[1], r[1] + j + 1)
                        dve.reciprocal(rin[:, :, j:j + 1], rs[:, :, j:j + 1]).then_inc(rin_done, 1)
                    j = i - 3
                    if 0 <= j < nh:
                        dve.wait_ge(m_ready[3], f[3] + j + 1)
                        dve.wait_ge(rin_done, (0 if name == "mla" else H) + j + 1)
                        dve.tensor_tensor(hn[:, :, j * HD:(j + 1) * HD],
                                          M[:, 3, 0:2 * HD].rearrange("p (t d) -> p t d", t=NT),
                                          rin[:, :, j:j + 1].to_broadcast([P, NT, HD]), ALU.mult)\
                           .then_inc(m_read[3], 1)
                return step

            def rest_o(name):
                for b in range(4):
                    dve.wait_ge(oh_done, OH[name] + b + 1)
                    dve.tensor_tensor(xl[:, 2 * b:2 * b + 2, :], pair(M[:, b, :]),
                                      xh[:, 2 * b:2 * b + 2, :].bitcast(F32), ALU.subtract)\
                       .then_inc(m_read[b], 1)

            step = heads("mla", H, DQ, 1)
            for i in range(H + 3):
                step(i)
            rest_o("mla")
            split_to(g + 12 + 3)
            residual(q + 9, g + 12, 1.0)
            scale_rows(2)
            rest_x("n2", 2)
            ffn("f1")

            def ple(name, nname, r):
                g, q, _, _ = PLAN[name]
                scale_rows(r)
                split_to(g + 1 + 3)
                rest_x(nname, r)
                split_to(g + 4 + 3)
                for t in range(NT):
                    for n in range(2):
                        fill = q + 2 + n
                        dve.wait_ge(acc_read[fill % 2], acc_reads(fill) - 1 + t)
                        dve.wait_ge(acc_read[(q + n) % 2], acc_reads(q + n))
                        cols = slice(512 * n, 512 * n + 512)
                        link(dve.tensor_tensor(gate[:, t, cols], gate[:, t, cols], pp[:, t, cols], ALU.mult))
                        e = dve.tensor_tensor(h[:, t, cols], h[:, t, cols], gate[:, t, cols], ALU.add)
                        if n:
                            e.then_inc(h_added, 1)

            ple("p0", "n3", 3)
            scale_rows(4)
            rest_x("n4", 4)
            ffn("f2")

            scale_rows(5)
            rest_x("n5", 5)
            g, q, f, r = PLAN["fox"]
            split_to(g + 3)
            for t in range(NT):
                tile_ready(dve, q, t, g)
                dve.tensor_tensor(fl[:, 0, t, :], acc(q, t)[:, 0:H], bf[:, :], ALU.add)\
                   .then_inc(acc_read[q % 2], 1)
            dve.wait_ge(forget_exp, 3)
            for t in range(NT):
                dve.scalar_tensor_tensor(fl[:, 2, t, :], fl[:, 0, t, :], 0.0, fl[:, 1, t, :],
                                         ALU.min, ALU.subtract).then_inc(forget_in, 1)
            qf = qn[:, :, 0:H * DF].rearrange("p t (h d) -> p t h d", d=DF)
            kf = kn[:, :, 0:H * DF].rearrange("p t (h d) -> p t h d", d=DF)
            for c in range(4):
                e = g + 2 + 2 * c
                fill = q + 1 + c
                split_to(e + 2)
                for t in range(NT):
                    dve.wait_ge(heads_sq, 4 + 2 * c + t + 1)
                    dve.tensor_reduce(hss[:, t, 0:8], heads3(sqb[:, t, 0:512], HD), AX, ALU.add)\
                       .then_inc(heads_ss, 1)
                split_to(e + 3)
                dst = (qf, kf)[c // 2]
                for t in range(NT):
                    dve.wait_ge(heads_rstd, 4 + 2 * c + t + 1)
                    dve.tensor_tensor(dst[:, t, 8 * (c % 2):8 * (c % 2) + 8, 0:HD], heads3(acc(fill, t), HD),
                                      hrs[:, t, 0:8].unsqueeze(2).to_broadcast([P, 8, HD]), ALU.mult)\
                       .then_inc(acc_read[fill % 2], 1)
                if c == 1:
                    dve.wait_ge(m_ready[3], f[3] + 1)
                    dec = M[:, 3, 0:2 * H].rearrange("p (t h) -> p t h", t=NT)
                    dve.memset(qf[:, :, :, HD + 1], 1.0)
                    dve.memset(kf[:, :, :, HD], 1.0)
                    dve.tensor_copy(qf[:, :, :, HD], dec)
                    dve.tensor_scalar(kf[:, :, :, HD + 1], dec, -1.0, None, ALU.mult).then_inc(m_read[3], 1)
            for c in range(4, 6):
                split_to(g + 2 + 2 * c + 3)
            split_to(g + 17)
            step = heads("fox", H, DF, 3)
            for i in range(H + 3):
                step(i)
            rest_o("fox")
            split_to(g + 16 + 3)
            residual(q + 7, g + 16, 1.0)
            scale_rows(6)
            rest_x("n6", 6)
            ffn("f3")
            ple("p1", "n7", 7)

            scale_rows(8)
            rest_x("n8", 8)
            g, q, _, _ = PLAN["b2"]
            hf, hr = HEADS["b2"]

            def b2_step(i):
                if i < NH2:
                    dve.wait_ge(m_ready[0], hf[0] + i + 1)
                    if i >= 2:
                        dve.wait_ge(m_ready[1], hf[1] + i - 1)
                    dve.wait_ge(m_read[0], hr[0] + 2 * i + 1)
                    dve.tensor_copy(qkT2[:, i % 2, S:2 * S], M[0:HD, 0, S:2 * S]).then_inc(m_read[0], 1)
                j = i - 1
                if 0 <= j < NH2:
                    dve.wait_ge(m_ready[1], hf[1] + j + 1)
                    dve.wait_ge(win_in[j % 2], 16 * (j // 2 + 1))
                    if j:
                        dve.wait_ge(m_ready[2], hf[2] + j)
                    for t in range(NT):
                        e = dve.tensor_tensor_reduce(pr2[:, t * S:(t + 1) * S], M[:, 1, t * S:(t + 1) * S],
                                                     win[:, j % 2, P - t * P:P - t * P + S], 1.0, -3.0e38,
                                                     ALU.add, ALU.max, mxp[:, t:t + 1])
                    e.then_inc(m_read[1], 1)
                    dve.wait_ge(m_read[1], hr[1] + j + 1)
                    dve.tensor_scalar(nmx[:, :, j], mxp[:, :], -1.0, None, ALU.mult).then_inc(max_done, 1)
                j = i - 2
                if 0 <= j < NH2:
                    dve.wait_ge(m_ready[2], hf[2] + j + 1)
                    if j:
                        dve.wait_ge(m_ready[3], hf[3] + j)
                    dve.tensor_copy(pT2[:, :], M[:, 2, :]).then_inc(m_read[2], 1)
                j = i - 3
                if 0 <= j < NH2:
                    dve.wait_ge(m_ready[3], hf[3] + j + 1)
                    dve.tensor_copy(oraw[:, :, j * HD:(j + 1) * HD],
                                    M[:, 3, 0:2 * HD].rearrange("p (t d) -> p t d", t=NT))\
                       .then_inc(m_read[3], 1)

            inner = 0
            at = 0
            for c, (what, j) in enumerate(B2_CHUNKS):
                fill = q + B2_FILL[c]
                for k in range(2):
                    w = 2 * c + k
                    split_to(g + w + 3)
                    if k == 1:
                        for t in range(NT):
                            if what in ("k", "a_in"):
                                tile_ready(dve, fill, t, g + w)
                                dve.tensor_copy(qkv[:, j % 2, 1, t, :] if what == "k" else u[:, t, :],
                                                acc(fill, t)).then_inc(acc_read[fill % 2], 1)
                            elif what in ("a_gate", "b_gp"):
                                inner += 1
                                dve.wait_ge(inner_exp, inner)
                                dst = (s_a if what == "a_gate" else s_b)[:, t, :]
                                link(dve.tensor_scalar(dst, et[:, :], 1.0, None, ALU.add))
                                dve.reciprocal(dst, dst).then_inc(gate_sum, 1)
                                dve.wait_ge(gate_sum, inner)
                                dve.tensor_tensor(dst, acc(fill, t), dst, ALU.mult)\
                                   .then_inc(acc_read[fill % 2], 1)
                            elif what == "g":
                                tile_ready(dve, fill, t, g + w)
                                dve.wait_ge(bg_in[j % 2], 16 * (j // 2 + 1))
                                dve.tensor_tensor(gts[:, t, 512 * j:512 * j + 512], acc(fill, t),
                                                  bg[:, j % 2, :], ALU.add).then_inc(acc_read[fill % 2], 1)
                    if w >= B2_HEAD0:
                        b2_step(at)
                        at += 1
                if what == "g":
                    for t in range(NT):
                        dve.wait_ge(gate_exp, 2 * j + t + 1)
                        part = gts[:, t, 512 * j:512 * j + 512]
                        link(dve.tensor_scalar(part, part, 1.0, None, ALU.add))
                        link(dve.reciprocal(part, part))
                if c == 9:
                    pf = q + B2_MIX
                    for t in range(NT):
                        tile_ready(dve, pf, t, None)
                        dve.tensor_tensor(s_a[:, t, :], acc(pf, t), s_a[:, t, :], ALU.mult)\
                           .then_inc(acc_read[pf % 2], 1)
            b2_step(at)

            pf = q + B2_YAT
            for k in range(4):
                if k % 2 == 0:
                    dve.wait_ge(oh_done, OH["b2"] + k + 2)
                e = dve.scalar_tensor_tensor(xl[:, k, :], acc(pf, k // 2)[:, (k % 2) * S:(k % 2 + 1) * S],
                                             gains[:, G_POOL + k:G_POOL + k + 1], xh[:, k, :].bitcast(F32),
                                             ALU.mult, ALU.subtract)
                if k % 2:
                    e.then_inc(acc_read[pf % 2], 1)

            groups = lambda ap: ap.rearrange("p t (g h) -> p t g h", g=G3)
            nm, sm = groups(nmx[:, :, :]), groups(rs[:, :, :])
            low = cmb[:, 0, 0:NT * H8].rearrange("p (t h) -> p t h", t=NT)
            den = cmb[:, 3, 0:NT * H8].rearrange("p (t h) -> p t h", t=NT)
            c_in, c_e = (cmb[:, n, :].rearrange("p (t g h) -> p t g h", t=NT, g=G3) for n in (1, 2))
            dve.wait_ge(exp_done, NH2)
            dve.wait_ge(m_read[3], hr[3] + NH2)
            link(dve.tensor_tensor(low, nm[:, :, 0, :], nm[:, :, 1, :], ALU.min))
            link(dve.tensor_tensor(low, low, nm[:, :, 2, :], ALU.min))
            for j in range(G3):
                e = dve.tensor_tensor(c_in[:, :, j, :], low, nm[:, :, j, :], ALU.subtract)
            e.then_inc(combine_in, 1)
            dve.wait_ge(combine_exp, 1)
            link(dve.tensor_tensor(c_in, c_e, sm, ALU.mult))
            link(dve.tensor_tensor(den, c_in[:, :, 0, :], c_in[:, :, 1, :], ALU.add))
            link(dve.tensor_tensor(den, den, c_in[:, :, 2, :], ALU.add))
            link(dve.reciprocal(den, den))
            for j in range(G3):
                link(dve.tensor_tensor(c_in[:, :, j, :], c_e[:, :, j, :], den, ALU.mult))
            for j in range(G3):
                dst = orev if j == 0 else otmp
                for t in range(NT):
                    link(dve.tensor_tensor(dst[:, t, :].rearrange("p (h d) -> p h d", d=HD),
                                           oraw[:, t, 512 * j:512 * j + 512].rearrange("p (h d) -> p h d", d=HD),
                                           c_in[:, t, j, :].unsqueeze(2).to_broadcast([P, H8, HD]), ALU.mult))
                if j:
                    e = dve.tensor_tensor(orev[:, :, :], orev[:, :, :], otmp[:, :, :], ALU.add)
                    if j == G3 - 1:
                        e.then_inc(o_done, 1)
                    else:
                        link(e)

            for t in range(NT):
                for n in range(2):
                    tile_ready(dve, q + B2_PA + n, t, g + 33)
                    dve.tensor_tensor(mg[:, t, 512 * n:512 * n + 512], acc(q + B2_PA + n, t),
                                      gts[:, t, 512 * n:512 * n + 512], ALU.mult)\
                       .then_inc(acc_read[(q + B2_PA + n) % 2], 1)
            split_to(g + 36)
            pf = q + B2_PERM
            for t in range(NT):
                tile_ready(dve, pf, t, None)
                dve.tensor_tensor(otmp[:, t, :], acc(pf, t), s_b[:, t, :], ALU.mult)\
                   .then_inc(acc_read[pf % 2], 1)
            pf = q + B2_YBT
            for b in range(2):
                dve.wait_ge(oh_done, OH["b2"] + 4 + b + 1)
                dve.tensor_tensor(xl[:, 4 + 2 * b:6 + 2 * b, :], pair(acc(pf, b)),
                                  xh[:, 4 + 2 * b:6 + 2 * b, :].bitcast(F32), ALU.subtract)\
                   .then_inc(acc_read[pf % 2], 1)
            split_to(g + 38)
            for t in range(NT):
                for n in range(2):
                    fill = q + B2_PB + n
                    tile_ready(dve, fill, t, g + 35)
                    cols = slice(512 * n, 512 * n + 512)
                    dve.tensor_tensor(orev[:, n, :], acc(fill, t), gts[:, t, D + 512 * n:D + 512 * n + 512],
                                      ALU.mult).then_inc(acc_read[fill % 2], 1)
                    dve.wait_ge(acc_read[fill % 2], acc_reads(fill) - 1 + t)
                    e = dve.tensor_tensor(mg[:, t, cols], mg[:, t, cols], orev[:, n, :], ALU.add)
            e.then_inc(mg_done, 1)
            for n in range(4):
                pf = q + B2_MT + n // 2
                dve.wait_ge(oh_done, OH["b2"] + 6 + n + 1)
                dve.tensor_tensor(xl[:, 2 * n:2 * n + 2, :], pair(acc(pf, n % 2)),
                                  xh[:, 2 * n:2 * n + 2, :].bitcast(F32), ALU.subtract)\
                   .then_inc(acc_read[pf % 2], 1)
            split_to(g + 40)
            residual(q + B2_OUT, g + 39, 1.0)
            dve.wait_ge(fg_in, 16)
            for t in range(NT):
                dve.wait_ge(rstd_done, NT * 9 + t + 1)
                dve.scalar_tensor_tensor(hn[:, t, :], h[:, t, :], rstd[:, t:t + 1], fg[:, :],
                                         ALU.mult, ALU.mult).then_inc(y_done, 1)

        @block.gpsimd
        def _(pool):
            steps = [0]

            def link(ins):
                steps[0] += 1
                ins.then_inc(p_step, 1)
                pool.wait_ge(p_step, steps[0])

            def inverse_rms(dst, src, n, width, signal):
                link(pool.tensor_scalar(dst, src, 1.0 / width, EPS, ALU.mult, ALU.add))
                pool.tensor_tensor(dst, dst, mhalf[:, 0:n], ALU.pow).then_inc(signal, 1)

            def norm(r):
                for t in range(NT):
                    pool.wait_ge(sq_done, NT * r + t + 1)
                    inverse_rms(rstd[:, t:t + 1], ssq[:, t:t + 1], 1, D, rstd_done)

            link(pool.memset(mhalf[:, :], -0.5))
            norm(0)
            norm(1)
            for c, width in enumerate((QR, KVR)):
                for t in range(NT):
                    pool.wait_ge(lat_sq, t + 1 if c == 0 else 2 + 2 * t + 1)
                    inverse_rms(lrs[:, c, t:t + 1], lss[:, c, t:t + 1], 1, width, lat_rstd)
            for n in range(4):
                pool.wait_ge(heads_ss, n + 1)
                inverse_rms(hrs[:, n, :], hss[:, n, :], H, DQ, heads_rstd)
                if n in (1, 2):
                    t = n - 1
                    pool.wait_ge(heads_scaled, t + 1)
                    qv = qn[:, t, :].rearrange("p (h d) -> p h d", d=DQ)
                    tb = [tab[:, 0, t, c, :].unsqueeze(1).to_broadcast([P, H, 16]) for c in range(4)]
                    x1, x2 = qv[:, :, NOPE:NOPE + 16], qv[:, :, NOPE + 16:DQ]
                    for m, (x, c) in enumerate(((x1, 0), (x2, 1), (x1, 2), (x2, 3))):
                        link(pool.tensor_tensor(rt[:, m, :, :], x, tb[c], ALU.mult))
                    link(pool.tensor_tensor(x1, rt[:, 0, :, :], rt[:, 1, :, :], ALU.subtract))
                    pool.tensor_tensor(x2, rt[:, 2, :, :], rt[:, 3, :, :], ALU.add).then_inc(q_rotated, 1)
            pool.wait_ge(m_ready[3], PLAN["n2"][2][3])
            pool.wait_ge(table_out, 16)
            pool.dma_start(p_n[:, :, :], I["p"][0, 0].rearrange("(t p) n -> p t n", p=P)).then_inc(p_in, 16)
            for r in range(2, 6):
                norm(r)
            for c in range(4):
                for t in range(NT):
                    pool.wait_ge(heads_ss, 4 + 2 * c + t + 1)
                    inverse_rms(hrs[:, t, 0:8], hss[:, t, 0:8], 8, HD, heads_rstd)
            pool.wait_ge(m_ready[3], PLAN["n6"][2][3])
            pool.dma_start(p_n[:, :, :], I["p"][1, 0].rearrange("(t p) n -> p t n", p=P)).then_inc(p_in, 16)
            for r in range(6, 9):
                norm(r)

            q = PLAN["b2"][1]
            hr = HEADS["b2"][1]
            pool.wait_ge(h_added, 2 * NT)
            pool.dma_start(bands[:, :, :, :], I["c_bands"]).then_inc(b2_small, 16)
            pool.dma_start(wp[:, :, :], I["w_pool_2"][0].rearrange("g c d -> c g d")).then_inc(b2_small, 16)

            def gate_bias(j):
                if j >= 2:
                    fill = q + B2_FILL[12 + j - 2]
                    pool.wait_ge(acc_read[fill % 2], acc_reads(fill))
                pool.dma_start(bg[:, j % 2, :], bass.AP(I["b_gate_2"].tensor, 512 * j, [[0, P], [1, 512]]))\
                    .then_inc(bg_in[j % 2], 16)

            gate_bias(0)
            gate_bias(1)
            pool.wait_ge(table_out, 16)
            for j in range(NH2):
                if j >= 2:
                    pool.wait_ge(m_read[1], hr[1] + j - 1)
                pool.dma_start(win[:, j % 2, :], bass.AP(scratch, 512 * j, [[1, P], [1, WIN]]))\
                    .then_inc(win_in[j % 2], 16)
            gate_bias(2)
            gate_bias(3)
            pool.wait_ge(m_ready[3], HEADS["b2"][0][3] + NH2)
            pool.dma_start(fg[:, :], bass.AP(I["final_gain_2"].tensor, 0, [[0, P], [1, D]])).then_inc(fg_in, 16)
            norm(9)


def constants():
    i = np.arange(P)
    mats = np.zeros((4, P, P), np.float32)
    mats[0] = np.eye(P)
    mats[1] = np.eye(P)[::-1]
    mats[2] = i[:, None] <= i[None, :]
    mats[3] = np.where(i[None, :] > i[:, None], np.float32(NEG), np.float32(0))
    onehot = np.zeros((33, G3, 512), np.float32)
    for g, (window, dil) in enumerate(DILATED):
        for m in range(512):
            off = m - (S - 1)
            n = abs(off)
            if off % dil or n > window // 2:
                onehot[32, g, m] = 1
                continue
            large = 8 + int(np.float32(np.log(np.float32(max(n, 1)) / np.float32(8)) / np.float32(np.log(128.0)) * 8))
            onehot[(16 if off > 0 else 0) + (n if n < 8 else min(large, 15)), g, m] = 1
    bands = np.zeros((P, NT, 4, S), np.float32)
    for g, w in enumerate(POOL_WINDOWS):
        for t in range(S):
            lo, hi = max(t - w // 2, 0), min(t + w // 2 - 1, S - 1)
            for s in range(lo, hi + 1):
                bands[s % P, s // P, g, t] += np.float32(1) / np.float32(hi - lo + 1)
            bands[t % P, t // P, g, t] -= 1
    freq = (np.float32(10000.0) ** (-np.arange(0, ROPE, 2, dtype=np.float32) / ROPE)).astype(np.float32)
    return {"c_mats": mats, "c_onehot": onehot.reshape(33, G3 * 512), "c_bands": bands, "c_freq": freq}


_AS_IS = ["x", "p", "ffn1_w_in", "ffn1_w_out", "ffn2_w_in", "ffn2_w_out", "ple_w_proj", "ple_w_gate", "mla_w_in",
          "mla_w_uq", "mla_w_ukv", "mla_w_o", "fox_w_in", "fox_b_f", "fox_w_o", "w_in_2", "b_gate_2",
          "rel_bias_2", "w_pool_2", "w_proj_a_2", "w_proj_b_2", "w_out_2", "final_gain_2"]
_OUTS = [((1, S, D), "float32")]


def kernel(**inputs):
    import concourse.bacc as _bacc
    from concourse.bass_utils import run_bass_kernel_spmd as _run

    def per_feature(v):
        return np.asarray(v).reshape(-1, P).T

    arrays = {n: np.ascontiguousarray(inputs[n]) for n in _AS_IS}
    arrays["gains"] = np.ascontiguousarray(np.concatenate(
        [per_feature(inputs[n][i]) for i in range(2) for n in ("g_ffn1", "g_mix", "g_ffn2", "g_ple")]
        + [per_feature(inputs[n]) for n in ("mla_g_q_lat", "mla_g_kv_lat", "norm_gain_2", "pool_scale_2")], axis=1))
    arrays["head_gains"] = np.ascontiguousarray(np.stack(
        [np.asarray(inputs[n])[0, :HD] for n in ("mla_g_qn", "mla_g_kn", "fox_g_qn", "fox_g_kn")], axis=1))
    arrays["rope_gains"] = np.ascontiguousarray(np.stack(
        [np.asarray(inputs[n])[0, NOPE:] for n in ("mla_g_qn", "mla_g_kn")]))
    arrays["pos"] = np.ascontiguousarray(np.asarray(inputs["positions"])[0].reshape(NT, P).T)
    arrays.update(constants())

    nc = _bacc.Bacc("TRN2", target_bir_lowering=False, num_devices=1)
    feed, I = {}, {}
    for name, a in arrays.items():
        feed[f"in_{name}_dram"] = a
        I[name] = nc.dram_tensor(f"in_{name}_dram", a.shape, mybir.dt.from_np(a.dtype), kind="ExternalInput").ap()
    out = nc.dram_tensor("out_0_dram", _OUTS[0][0], F32, kind="ExternalOutput").ap()
    build(nc, I, out)
    r = _run(nc, [feed], core_ids=[0])
    return r.results[0]["out_0_dram"]
```

```python
from contextlib import ExitStack

import numpy as np
import concourse.bass as bass
from concourse import mybir

F32 = mybir.dt.float32
F32R = mybir.dt.float32r
BF16 = mybir.dt.bfloat16
I32 = mybir.dt.int32
ALU = mybir.AluOpType
ACT = mybir.ActivationFunctionType
AX = mybir.AxisListType.X

P = 128
S = 256
NT = S // P
D = 1024
DK = D // P
FF = 2816
FCH = FF // 256
PLE = 256
H = 16
QR, KVR, ROPE, NOPE = 512, 256, 32, 64
DQ = NOPE + ROPE
LAT = QR + KVR + ROPE
HD = 64
DF = HD + 2
G3, H8 = 3, 8
NH2 = G3 * H8
WIN = 3 * P
EPS = 1e-6
RING = 4
GC = 2048
NEG = -1.0e30
DILATED = ((128, 1), (512, 4), (2048, 16))
POOL_WINDOWS = (2, 4, 8, 16)

G_LAYER, G_QLAT, G_KVLAT, G_NORM2, G_POOL = 32, 64, 68, 70, 78
NORM_GAIN = [0, 8, 16, 24, 32, 40, 48, 56, G_NORM2]

B2_CHUNKS = [("q", 0), ("k", 0), ("v", 0), ("q", 1), ("k", 1), ("v", 1), ("a_in", 0), ("q", 2),
             ("k", 2), ("v", 2), ("a_gate", 0), ("b_gp", 0), ("g", 0), ("g", 1), ("g", 2), ("g", 3)]
B2_COL = {"a_in": 0, "a_gate": 512, "q": 1024, "k": 2560, "v": 4096, "b_gp": 5632, "g": 6144}
B2_FILL = [0, 1, 2, 3, 4, 5, 6, 7, 8, 9, 10, 12, 14, 16, 18, 20]
B2_POOL, B2_MIX, B2_PERM, B2_YAT, B2_YBT, B2_PA, B2_PB, B2_OUT = 11, 13, 15, 17, 19, 21, 23, 25
B2_QKV = [(0, 1, 2), (3, 4, 5), (7, 8, 9)]
B2_STEPS = [0] * 6 + [1] * 14 + [3, 1, 3, 1, 2, 2] + [1] + [0] * 5
B2_COMBINE = 26


def plan():
    sizes = {
        "norm": (0, 0, (1, 1, 1, 1), (4, 4, 4, 4)),
        "ffn": (33, 13, (6, 5, 0, 0), (6, 5, 0, 0)),
        "ffn_t": (33, 13, (6, 5, 0, G3), (6, 5, 0, G3)),
        "ffn_p": (33, 13, (6, 5, 1, 0), (6, 5, 1, 0)),
        "mla": (14, 12 + H, (H // 2 + 2, H // 2 + 2, H + 2, H + 1), (H + 2, H + 2, H + 2, H + 1)),
        "fox": (17, 9 + H, (H // 2 + 1, H // 2 + 1, H + 1, H + 2), (H + 1, H + 1, H + 1, H + 2)),
        "ple": (5, 4, (0, 0, 0, 0), (0, 0, 0, 0)),
        "b2": (40, 27, (NH2,) * 4, (2 * NH2, NH2, NH2, NH2)),
    }
    order = [("n0", "norm"), ("f0", "ffn_t"), ("n1", "norm"), ("mla", "mla"), ("n2", "norm"),
             ("f1", "ffn_p"), ("n3", "norm"), ("p0", "ple"), ("n4", "norm"), ("f2", "ffn"), ("n5", "norm"),
             ("fox", "fox"), ("n6", "norm"), ("f3", "ffn_p"), ("n7", "norm"), ("p1", "ple"), ("n8", "norm"),
             ("b2", "b2")]
    g = q = 0
    f, r = [0] * 4, [0] * 4
    at = {}
    for name, kind in order:
        at[name] = (g, q, tuple(f), tuple(r))
        dg, dq, df, dr = sizes[kind]
        g, q = g + dg, q + dq
        f = [a + b for a, b in zip(f, df)]
        r = [a + b for a, b in zip(r, dr)]
    return at, g


PLAN, NGROUPS = plan()


def heads_at():
    before = {"mla": (1, 1, 1, 0), "fox": (0, 0, 0, 1), "b2": (0, 0, 0, 0)}
    return {n: tuple([a + b for a, b in zip(PLAN[n][x], before[n])] for x in (2, 3)) for n in before}


HEADS = heads_at()
TABLE_AT = (2, 4, 6)
S_FILL = {"mla": 10, "fox": 7}
OT_READS = {n: (HEADS[n][1][0] + H, HEADS[n][1][1] + H, HEADS[n][1][2] + H, HEADS[n][1][3] + H)
            for n in ("mla", "fox")}
OT_FILLS = {n: (HEADS[n][0][0] + H // 2, HEADS[n][0][1] + H // 2, HEADS[n][0][2] + H, HEADS[n][0][3] + H)
            for n in ("mla", "fox")}
B2_END = tuple(HEADS["b2"][1][b] + (2 * NH2 if b == 0 else NH2) for b in range(4))


def fox_fill(c):
    return c + (c > 0)


def build(nc, I, out):
    with ExitStack() as ctx:
        def sem(name):
            return ctx.enter_context(nc.semaphore(name))

        top = [0]

        def sb(name, shape, dt=F32):
            n = int(np.prod(shape[1:])) * (2 if dt == BF16 else 4)
            t = nc.alloc_sbuf_tensor_at(name, list(shape), dt, offset=BASE + top[0])
            top[0] += (n + 31) // 32 * 32
            return t

        BASE = (nc.sbuf_base + 63) // 64 * 64
        raw = sb("raw", [P, RING, GC])
        wh = sb("wh", [P, RING, GC], F32R)
        wl = sb("wl", [P, RING, GC], F32R)
        h = sb("h", [P, NT, D])
        hn = sb("hn", [P, NT, D])
        xh = sb("xh", [P, DK, S], F32R)
        xl = sb("xl", [P, DK, S], F32R)
        ident = sb("ident", [P, P])
        flip = sb("flip", [P, P])
        tri = sb("tri", [P, P])
        ones = sb("ones", [P, P])
        identb = sb("identb", [P, P], BF16)
        causal = sb("causal", [P, 2 * P], BF16)
        gains = sb("gains", [P, 82])
        headg = sb("headg", [P, 4])
        tab = sb("tab", [P, 2, NT, 4, 16])
        ssq = sb("ssq", [P, NT])
        rstd = sb("rstd", [P, NT])
        mhalf = sb("mhalf", [P, 32])
        lss = sb("lss", [P, 2, NT])
        lrs = sb("lrs", [P, 2, NT])
        kss = sb("kss", [P, NT])
        hss = sb("hss", [P, 4, H])
        hrs = sb("hrs", [P, 4, H])
        nmx = sb("nmx", [P, NT, NH2])
        rs = sb("rs", [P, NT, NH2])
        rin = sb("rin", [P, NT, NH2])
        bf = sb("bf", [P, H])
        mxp = sb("mxp", [P, 2, NT])
        fl = sb("fl", [P, 3, NT, H])
        XB = BASE + top[0]

        def region():
            at = [0]

            def x(name, shape, dt=F32, offset=None):
                n = int(np.prod(shape[1:])) * (2 if dt == BF16 else 4)
                o = at[0] if offset is None else offset
                at[0] = max(at[0], o + (n + 31) // 32 * 32)
                return nc.alloc_sbuf_tensor_at(name, list(shape), dt, offset=XB + o)
            return x

        x = region()
        ah = x("ah", [P, 2 * FCH, S], F32R)
        al = x("al", [P, 2 * FCH, S], F32R)
        sg = x("sg", [P, 2, NT, 256])
        a_n = x("a_n", [P, 2, NT, 256])
        p_n = x("p_n", [P, NT, PLE])
        ph = x("ph", [P, 2, S], F32R)
        pl = x("pl", [P, 2, S], F32R)
        pp = x("pp", [P, NT, D])
        x = region()
        gate = x("gate", [P, NT, D])
        x = region()
        qn = x("qn", [P, NT, H * DQ])
        kn = x("kn", [P, NT, H * DQ])
        vn = x("vn", [P, NT, H * HD])
        lat = x("lat", [P, NT, QR + KVR])
        o_l = NT * (H * DQ * 2 + H * HD + QR + KVR) * 4
        lh = x("lh", [P, 6, S], F32R)
        ll = x("ll", [P, 6, S], F32R)
        qkT = x("qkT", [P, 2, 2 * S], offset=o_l)
        probs = x("probs", [P, 2, 3 * P])
        pT = x("pT", [P, 2, 3 * P])
        sqb = x("sqb", [P, 2, H * DQ], offset=o_l + 12 * 1024)
        rt = x("rt", [P, 4, H, 16])
        kpe = x("kpe", [P, NT, ROPE])
        kpr = x("kpr", [P, NT, ROPE])
        x = region()
        x("below", [P, 1], offset=2 * (2 * FCH * S * 4) + 2 * (2 * NT * 256 * 4) - 32)
        causal_f = x("causal_f", [P, P])
        onehot = x("onehot", [33, G3 * 512])
        rb = x("rb", [33, NH2])
        tsb = x("tsb", [H8, G3, 512])
        hraw = x("hraw", [HD, 4])
        rgain = x("rgain", [P, 2, ROPE])
        freq = x("freq", [P, 16])
        posi = x("posi", [P, NT], I32)
        posf = x("posf", [P, NT])
        ang = x("ang", [P, NT, 16])
        turns = x("turns", [P, NT, 16])
        rc = x("rc", [P, 2, NT, 16])
        wrap = x("wrap", [P, NT, 16])
        cs = x("cs", [P, 2, NT, 16])
        x = region()
        qkv = x("qkv", [P, 2, 3, NT, 512])
        win = x("win", [P, 2, WIN])
        oraw = x("oraw", [P, NT, NH2 * HD])
        gts = x("gts", [P, NT, 2 * D])
        o_g = (2 * 3 * NT * 512 + 2 * WIN + NT * NH2 * HD) * 4
        bands = x("bands", [P, 2, 4, S], offset=o_g)
        u = x("u", [P, NT, 512], offset=o_g + 8 * 1024)
        plT = x("plT", [P, 4, S], offset=o_g + 12 * 1024)
        wp = x("wp", [P, 4, P], offset=o_g + 16 * 1024)
        qkT2 = x("qkT2", [HD, 2, 2 * S])
        pr2 = x("pr2", [P, 2 * S])
        pT2 = x("pT2", [P, 2 * S])
        bg = x("bg", [P, 4, 512])
        o_t = o_g + 16 * 1024 + 4 * P * 4
        yah = x("yah", [P, 4, S], F32R, offset=o_t)
        yal = x("yal", [P, 4, S], F32R, offset=o_t + 4 * S * 4)
        x = region()
        orev = x("orev", [P, NT, 512])
        otmp = x("otmp", [P, NT, 512])
        cmb = x("cmb", [P, 4, NT * NH2])
        x("gap", [P, 1], offset=12 * 1024 - 32)
        mg = x("mg", [P, NT, D])
        fg = x("fg", [P, D])
        o_r = (2 * 3 * NT * 512 + 2 * WIN) * 4
        ybh = x("ybh", [P, 4, S], F32R, offset=o_r)
        ybl = x("ybl", [P, 4, S], F32R)
        s_a = hn[:, 0, :].rearrange("p (t n) -> p t n", t=NT)
        s_b = hn[:, 1, :].rearrange("p (t n) -> p t n", t=NT)

        acc_t = ctx.enter_context(nc.psum_tensor("acc", [P, NT, 2, 512], F32))
        M = ctx.enter_context(nc.psum_tensor("misc", [P, 4, 512], F32))
        scratch = nc.dram_tensor("bias_by_offset", (NH2, 512), F32, kind="Internal")

        def acc(q, t):
            return acc_t[:, t, q % 2, :]

        x_in = [sem(f"x_in{t}") for t in range(NT)]
        ident_in = sem("ident_in")
        gains_in = sem("gains_in")
        small_in = sem("small_in")
        ph_done = sem("ph_done")
        oh_done = sem("oh_done")
        p_in = sem("p_in")
        raw_in = [sem(f"raw_in{i}") for i in range(RING)]
        hi_done = sem("hi_done")
        lo_done = sem("lo_done")
        w_used = sem("w_used")
        acc_ready = sem("acc_ready")
        acc_read = [sem(f"acc_read{i}") for i in range(2)]
        m_ready = [sem(f"m_ready{i}") for i in range(4)]
        m_read = [sem(f"m_read{i}") for i in range(4)]
        h_added = sem("h_added")
        sq_done = sem("sq_done")
        rstd_done = sem("rstd_done")
        xh_done = sem("xh_done")
        silu_done = sem("silu_done")
        ah_done = sem("ah_done")
        gate_done = sem("gate_done")
        lat_sq = sem("lat_sq")
        lat_rstd = sem("lat_rstd")
        lh_done = sem("lh_done")
        heads_sq = sem("heads_sq")
        heads_ss = sem("heads_ss")
        heads_rstd = sem("heads_rstd")
        heads_ready = sem("heads_ready")
        q_rotated = sem("q_rotated")
        max_done = sem("max_done")
        exp_done = sem("exp_done")
        rin_done = sem("rin_done")
        forget_exp = sem("forget_exp")
        forget_in = sem("forget_in")
        const_ready = sem("const_ready")
        table_out = sem("table_out")
        angles = sem("angles")
        sines = sem("sines")
        v_step = sem("v_step")
        p_step = sem("p_step")
        win_in = [sem(f"win_in{i}") for i in range(2)]
        biased = sem("biased")
        b2_small = sem("b2_small")
        combine_in = sem("combine_in")
        combine_exp = sem("combine_exp")
        shares = sem("shares")
        o_done = sem("o_done")
        mg_done = sem("mg_done")
        fg_in = sem("fg_in")
        y_done = sem("y_done")
        y_out = sem("y_out")

        def acc_reads(q):
            return 2 * (q // 2) + 2

        def tile_ready(eng, q, t, g, i=0, di=0):
            if t == 0 or g is None:
                eng.wait_ge(acc_ready, q + 1 + di * i)
            else:
                eng.wait_ge(w_used, g + 1 + 2 * di * i)

        def columns(g):
            gm, gx = PLAN["mla"][0], PLAN["fox"][0]
            if g in (gm, gm + 1):
                return 4 * (LAT - QR)
            if gm + 6 <= g < gm + 10:
                return 4 * 4 * DQ
            return DK * H if g == gx + 2 else GC

        block = ctx.enter_context(nc.Block())

        def copy_kv(eng, fill, t, n):
            src = acc(fill, t).rearrange("p (h d) -> p h d", d=NOPE + HD)
            dk = kn[:, t, :].rearrange("p (h d) -> p h d", d=DQ)[:, 4 * n:4 * n + 4, 0:NOPE]
            dv = vn[:, t, 4 * n * HD:4 * (n + 1) * HD].rearrange("p (h d) -> p h d", d=HD)
            for dst, part in ((dk, src[:, :, 0:NOPE]), (dv, src[:, :, NOPE:])):
                if eng is nc.scalar:
                    c = nc.scalar.activation(dst, part, ACT.Copy, scale=lrs[:, 1, t:t + 1])
                else:
                    c = nc.vector.tensor_scalar(dst, part, lrs[:, 1, t:t + 1], None, ALU.mult)
            c.then_inc(acc_read[fill % 2], 1)

        @block.sync
        def _(sp):
            def room(g, i=0):
                if g >= RING:
                    sp.wait_ge(lo_done, g - RING + 1 + RING * i)

            def fetch(g, parts, i=0):
                room(g, i)
                for dst, src in parts:
                    sp.dma_start(dst, src).then_inc(raw_in[g % RING], 16)

            def tall(g, w, row, col, n=512):
                dst = raw[:, g % RING, 0:4 * n].rearrange("p (k n) -> p k n", k=4)
                src = w[row:row + 512, col:col + n].rearrange("(k p) n -> p k n", p=P)
                fetch(g, [(dst[:, 2 * j:2 * j + 2, :], src[:, 2 * j:2 * j + 2, :]) for j in range(2)])

            def wide(g, w, row, col=0):
                dst = raw[:, g % RING, :].rearrange("p (k n) -> p k n", k=2)
                src = w[row:row + 256, col:col + D].rearrange("(k p) n -> p k n", p=P)
                fetch(g, [(dst[:, j:j + 1, :], src[:, j:j + 1, :]) for j in range(2)])

            def gate_up(g, w, k, c, i=0):
                dst = raw[:, g % RING, :].rearrange("p (k u n) -> p k u n", k=4, u=2)
                fetch(g, [(dst[:, :, j, :], w[512 * k:512 * k + 512, bass.ds(c * 256 + j * FF, 256)]
                           .rearrange("(k p) n -> p k n", p=P)) for j in range(2)], i)

            def ffn(name, w_in, w_out):
                g0 = PLAN[name][0]
                peel = 3 if g0 == 0 else 1
                for c in range(peel):
                    for k in range(2):
                        gate_up(g0 + 2 * c + k, w_in, k, c)
                        if g0 + c + k == 0:
                            load_x(1)
                with sp.Fori(0, (FCH - peel) // 2) as i:
                    for c in range(2):
                        for k in range(2):
                            gate_up(g0 + 2 * (peel + c) + k, w_in, k, i * 2 + peel + c, i)
                for c in range(FCH):
                    wide(g0 + 2 * FCH + c, w_out, 256 * c)

            def load_x(t):
                sp.dma_start(h[:, t, :], I["x"][0, t * P:(t + 1) * P, :]).then_inc(x_in[t], 16)

            load_x(0)
            ffn("f0", I["ffn1_w_in"][0], I["ffn1_w_out"][0])
            g = PLAN["mla"][0]
            for k in range(2):
                tall(g + k, I["mla_w_in"][0], 512 * k, QR, LAT - QR)
            for k in range(2):
                tall(g + 2 + k, I["mla_w_in"][0], 512 * k, 0)
            for c in range(2):
                wide(g + 4 + c, I["mla_w_ukv"][0], 0, D * c)
            for c in range(4):
                tall(g + 6 + c, I["mla_w_uq"][0], 0, 4 * DQ * c, 4 * DQ)
            for k in range(4):
                wide(g + 10 + k, I["mla_w_o"][0], 256 * k)
            ffn("f1", I["ffn2_w_in"][0], I["ffn2_w_out"][0])

            def ple(name, i):
                g = PLAN[name][0]
                wide(g, I["ple_w_proj"][i], 0)
                for k in range(4):
                    wide(g + 1 + k, I["ple_w_gate"][i], 256 * k)

            ple("p0", 0)
            ffn("f2", I["ffn1_w_in"][1], I["ffn1_w_out"][1])
            g = PLAN["fox"][0]
            for c in range(6):
                for k in range(2):
                    tall(g + 2 * c + k + (c > 0), I["fox_w_in"][0], 512 * k, 512 * c)
                if c == 0:
                    dst = raw[:, (g + 2) % RING, 0:DK * H].rearrange("p (k n) -> p k n", k=DK)
                    src = I["fox_w_in"][0][:, 3 * D:3 * D + H].rearrange("(k p) n -> p k n", p=P)
                    fetch(g + 2, [(dst[:, 4 * j:4 * j + 4, :], src[:, 4 * j:4 * j + 4, :]) for j in range(2)])
            for k in range(4):
                wide(g + 13 + k, I["fox_w_o"][0], 256 * k)
            ffn("f3", I["ffn2_w_in"][1], I["ffn2_w_out"][1])
            ple("p1", 1)
            g = PLAN["b2"][0]
            for c, (what, j) in enumerate(B2_CHUNKS):
                for k in range(2):
                    tall(g + 2 * c + k, I["w_in_2"][0], 512 * k, B2_COL[what] + 512 * j)
            for n, (w, ks) in enumerate([("w_proj_a_2", 2), ("w_proj_b_2", 2), ("w_out_2", 4)]):
                for k in range(ks):
                    wide(g + 32 + 2 * n + k, I[w][0], 256 * k)
            for t in range(NT):
                sp.wait_ge(y_done, t + 1)
                sp.dma_start(out[0, t * P:(t + 1) * P, :], hn[:, t, :]).then_inc(y_out, 16)
            sp.wait_ge(y_out, 16 * NT)

        def rows_ready(eng, r, t):
            if r == 0:
                eng.wait_ge(x_in[t], 16)
            elif r in (4, 8):
                eng.wait_ge(h_added, NT * (r // 4 - 1) + t + 1)
            else:
                q = {1: PLAN["f0"][1] + 12, 2: PLAN["mla"][1] + 11 + H, 3: PLAN["f1"][1] + 12,
                     5: PLAN["f2"][1] + 12, 6: PLAN["fox"][1] + 8 + H, 7: PLAN["f3"][1] + 12,
                     9: PLAN["b2"][1] + B2_OUT + 1}[r]
                eng.wait_ge(acc_read[q % 2], acc_reads(q) - 1 + t)

        SMALL = 10
        FIRST_SILU = {"f0": 0, "f1": 1, "f2": 2, "f3": 3}
        OH = {"mla": 0, "fox": 4, "b2": 8}

        @block.tensor
        def _(pe):
            def wait_group(g, i=0):
                pe.wait_ge(lo_done, g + 1 + RING * i)

            def open_acc(q, i=0):
                if q >= 2:
                    pe.wait_ge(acc_read[q % 2], acc_reads(q - 2) + 2 * i)

            def open_tile(q, t):
                if q >= 2:
                    pe.wait_ge(acc_read[q % 2], acc_reads(q - 2) - 1 + t)

            def open_m(b, reads):
                if reads:
                    pe.wait_ge(m_read[b], reads)

            def products(dst, hi, lo, rhs_h, rhs_l, first, last):
                pe.matmul(dst, hi, rhs_h, start=first, stop=False)
                pe.matmul(dst, hi, rhs_l, start=False, stop=False)
                return pe.matmul(dst, lo, rhs_h, start=False, stop=last)

            def tall_group(g, q, ah_, al_, k0, kts, n, first, last):
                s = g % RING
                for k in range(kts):
                    for t in range(NT):
                        mm = products(acc(q, t)[:, 0:n], ah_[:, k0 + k, t * P:(t + 1) * P],
                                      al_[:, k0 + k, t * P:(t + 1) * P],
                                      wh[:, s, k * n:(k + 1) * n], wl[:, s, k * n:(k + 1) * n],
                                      first and k == 0, last and k == kts - 1)
                        if last and t == 0 and k == kts - 1:
                            mm.then_inc(acc_ready, 1)
                mm.then_inc(w_used, 1)

            def wide_tile(g, q, t, ah_, al_, k0, first, last, between=None, x_wait=None):
                s = g % RING
                for k in range(2):
                    if x_wait:
                        x_wait(t, k0 + k)
                    if between and k == 1:
                        between()
                    xa = ah_[:, k0 + k, t * P:(t + 1) * P]
                    xb = al_[:, k0 + k, t * P:(t + 1) * P]
                    st, en = first and k == 0, last and k == 1
                    for n in range(2):
                        r = slice(k * D + n * 512, k * D + (n + 1) * 512)
                        pe.matmul(acc(q + n, t), xa, wh[:, s, r], start=st, stop=False)
                        pe.matmul(acc(q + n, t), xa, wl[:, s, r], start=False, stop=False)
                    for n in range(2):
                        r = slice(k * D + n * 512, k * D + (n + 1) * 512)
                        mm = pe.matmul(acc(q + n, t), xb, wh[:, s, r], start=False, stop=en)
                        if en and t == 0:
                            mm.then_inc(acc_ready, 1)
                if t == NT - 1:
                    mm.then_inc(w_used, 1)

            def wide_stage(g0, q, ah_, al_, kts, k_first=0, x_wait=None, between=None, tiled=False):
                if not tiled:
                    open_acc(q)
                    open_acc(q + 1)
                last = kts // 2 - 1
                for t in range(NT):
                    if tiled:
                        open_tile(q, t)
                        open_tile(q + 1, t)
                    for j in range(last + 1):
                        if t == 0:
                            wait_group(g0 + j)
                        wide_tile(g0 + j, q, t, ah_, al_, k_first + 2 * j, j == 0, j == last,
                                  between if t and j == last else None, x_wait)

            def turn(b, cols, src, rows=P, m=ident):
                return pe.transpose(M[0:rows, b, cols], src, m[:, :])

            def turn_rows(name, t, rows=h, opened=None):
                rd = opened or PLAN[name][3]
                for b in (2 * t, 2 * t + 1):
                    open_m(b, rd[b])
                for k in range(DK):
                    o = (k // 2) * P
                    mm = turn(2 * t + k % 2, slice(o, o + P), rows[:, t, k * P:(k + 1) * P])
                    if k >= DK - 2:
                        mm.then_inc(m_ready[2 * t + k % 2], 1)

            def turn_h(name, r):
                def work():
                    rows_ready(pe, r, 0)
                    turn_rows(name, 0)
                return work

            def x_wait(name):
                rd = PLAN[name][3]
                return lambda t, k: pe.wait_ge(m_read[2 * t + k % 2], rd[2 * t + k % 2] + k // 2 + 1)

            def first_fill(name, r, g, q, n=512):
                ready = x_wait(name)
                for t in range(NT):
                    open_tile(q, t)
                    for k in range(DK):
                        if t == 0 and k % 4 == 0:
                            wait_group(g + k // 4)
                        if t == 0 and k == DK - 2:
                            rows_ready(pe, r, 1)
                            turn_rows(name, 1)
                        ready(t, k)
                        s, c = (g + k // 4) % RING, (k % 4) * n
                        mm = products(acc(q, t)[:, 0:n], xh[:, k, t * P:(t + 1) * P],
                                      xl[:, k, t * P:(t + 1) * P], wh[:, s, c:c + n], wl[:, s, c:c + n],
                                      k == 0, k == DK - 1)
                        if t == 0 and k == DK - 1:
                            mm.then_inc(acc_ready, 1)
                        if t == NT - 1 and k % 4 == 3:
                            mm.then_inc(w_used, 1)

            def ffn(name, nname, r, after, r_after, with_p=None):
                g0, q0, f0, r0 = PLAN[name]

                def chunk(c, i=0):
                    q, g = q0 + c, g0 + 2 * c
                    open_acc(q, i)
                    for k in range(2):
                        wait_group(g + k, i)
                        tall_group(g + k, q, xh, xl, 4 * k, 4, 512, k == 0, k == 1)
                        if k == 0:
                            turn_products(c - 1, i)

                def turn_products(c, i=0):
                    b, q = c % 2, q0 + c
                    pe.wait_ge(acc_read[q % 2], acc_reads(q) + 2 * i)
                    if r0[b] + c // 2 > 0:
                        pe.wait_ge(m_read[b], r0[b] + c // 2 + i)
                    for t in range(NT):
                        for k in range(2):
                            mm = turn(b, slice(k * S + t * P, k * S + (t + 1) * P),
                                      a_n[:, b, t, k * P:(k + 1) * P])
                    mm.then_inc(m_ready[b], 1)

                peel = 3 if g0 == 0 else 1
                first_fill(nname, r, g0, q0)
                for c in range(1, peel):
                    chunk(c)
                with pe.Fori(0, (FCH - peel) // 2) as i:
                    for c in range(2):
                        chunk(peel + c, i)
                q, g = q0 + FCH, g0 + 2 * FCH
                for c in range(FCH):
                    wait_group(g + c)
                    pe.wait_ge(m_read[c % 2], r0[c % 2] + c // 2 + 1)
                    for t in range(NT):
                        if c == 0:
                            open_tile(q, t)
                            open_tile(q + 1, t)
                        wide_tile(g + c, q, t, ah, al, 2 * c, c == 0, c == FCH - 1,
                                  turn_h(after, r_after) if t and c == FCH - 1 else None)
                    if c == 0:
                        turn_products(FCH - 1)
                        if with_p is not None:
                            open_m(2, r0[2])
                            pe.wait_ge(p_in, 16 * (with_p + 1))
                            for t in range(NT):
                                for k in range(2):
                                    mm = turn(2, slice(k * S + t * P, k * S + (t + 1) * P),
                                              p_n[:, t, k * P:(k + 1) * P])
                            mm.then_inc(m_ready[2], 1)
                    if g0 == 0 and c in TABLE_AT:
                        j = TABLE_AT.index(c)
                        pe.wait_ge(const_ready, 1)
                        open_m(3, r0[3] + j)
                        pe.matmul(M[0:H8, 3, :], rb[:, H8 * j:H8 * j + H8], onehot[:, 512 * j:512 * j + 512],
                                  start=True, stop=True).then_inc(m_ready[3], 1)

            def heads(name, nh, dk, q_of, k_of, v_of, qkT_, pr, pT_, ready, after, full=False):
                base = HEADS[name][1]
                sq = PLAN[name][1] + S_FILL.get(name, 0)

                def step(i):
                    if i < nh:
                        ready(i)
                        tb, tn = (0, i) if full else (i % 2, i // 2)
                        open_m(tb, base[tb] + 2 * tn)
                        for t in range(NT):
                            if full:
                                pe.matmul(M[0:dk, tb, t * P:(t + 1) * P], q_of(i, t), flip[:, :],
                                          start=True, stop=True)
                            else:
                                turn(tb, slice(t * P, (t + 1) * P), q_of(i, t), dk)
                        for t in range(NT):
                            mm = turn(tb, slice(S + t * P, S + (t + 1) * P), k_of(i, t), dk)
                        mm.then_inc(m_ready[tb], 1)
                    if 0 <= i - 1 < nh:
                        j = i - 1
                        tb, tn = (0, j) if full else (j % 2, j // 2)
                        pe.wait_ge(m_read[tb], base[tb] + 2 * tn + 2)
                        s = j % 2
                        qT, kT = qkT_[0:dk, s, 0:S], qkT_[0:dk, s, S:2 * S]
                        if full:
                            open_m(1, base[1] + j)
                            for t in range(NT):
                                mm = pe.matmul(M[:, 1, t * S:(t + 1) * S], qT[:, t * P:(t + 1) * P], kT,
                                               start=True, stop=True)
                            mm.then_inc(m_ready[1], 1)
                        else:
                            open_acc(sq + j)
                            sc = acc(sq + j, 0)
                            pe.matmul(sc[:, 0:P], qT[:, 0:P], kT[:, 0:P], start=True, stop=False)
                            pe.matmul(sc[:, 0:P], identb[:, :], causal[:, P:2 * P], start=False, stop=True)
                            pe.matmul(sc[:, P:3 * P], qT[:, P:S], kT, start=True, stop=False)
                            pe.matmul(sc[:, P:3 * P], identb[:, :], causal[:, :],
                                      start=False, stop=True).then_inc(acc_ready, 1)
                    if 0 <= i - 2 < nh:
                        j = i - 2
                        if full:
                            pe.wait_ge(exp_done, j + 1)
                        else:
                            pe.wait_ge(acc_read[(sq + j) % 2], acc_reads(sq + j))
                        open_m(2, base[2] + j)
                        src = pr if full else pr[:, j % 2]
                        for n in range(4 if full else 3):
                            mm = turn(2, slice(n * P, (n + 1) * P), src[:, n * P:(n + 1) * P])
                        mm.then_inc(m_ready[2], 1)
                    if 0 <= i - 3 < nh:
                        j = i - 3
                        pe.wait_ge(m_read[2], base[2] + j + 1)
                        open_m(3, base[3] + j)
                        src = pT_ if full else pT_[:, j % 2]
                        blocks = [[(0, 0), (1, 1)], [(2, 0), (3, 1)]] if full else [[(0, 0)], [(1, 0), (2, 1)]]
                        for t in range(NT):
                            for n, (col, kt) in enumerate(blocks[t]):
                                mm = pe.matmul(M[:, 3, t * HD:(t + 1) * HD], src[:, col * P:(col + 1) * P],
                                               v_of(j, kt), start=n == 0, stop=n == len(blocks[t]) - 1)
                        mm.then_inc(m_ready[3], 1)
                        after(j)
                return step

            def turn_o(name):
                rd = OT_READS[name]
                pe.wait_ge(m_read[3], rd[3])
                for t in range(NT):
                    turn_rows(name, t, hn, rd)

            def o_wait(name):
                rd = OT_READS[name]
                return lambda t, k: pe.wait_ge(m_read[2 * t + k % 2], rd[2 * t + k % 2] + 1)

            pe.wait_ge(ident_in, 16)
            rows_ready(pe, 0, 0)
            turn_rows("n0", 0)
            ffn("f0", "n0", 0, "n1", 1)

            g, q, f, r = PLAN["mla"]
            first_fill("n1", 1, g, q, LAT - QR)
            def turn_latents(ks, fill):
                pe.wait_ge(acc_read[fill % 2], acc_reads(fill))
                for k in ks:
                    if k % 2 == 0:
                        open_m(k // 2, r[k // 2])
                    for t in range(NT):
                        o = (k % 2) * S + t * P
                        mm = turn(k // 2, slice(o, o + P), lat[:, t, k * P:(k + 1) * P])
                    if k % 2:
                        mm.then_inc(m_ready[k // 2], 1)

            open_acc(q + 1)
            for k in range(2):
                wait_group(g + 2 + k)
                tall_group(g + 2 + k, q + 1, xh, xl, 4 * k, 4, QR, k == 0, k == 1)
                if k == 0:
                    turn_latents(range(4, 6), q)
            for c in range(2):
                wide_stage(g + 4 + c, q + 2 + 2 * c, lh, ll, 2, 4,
                           (lambda t, k: pe.wait_ge(m_read[2], r[2] + 1)) if c == 0 else None,
                           None, c == 0)
                if c == 0:
                    turn_latents(range(4), q + 1)
            for c in range(4):
                open_acc(q + 6 + c)
                wait_group(g + 6 + c)
                if c == 0:
                    pe.wait_ge(m_read[0], r[0] + 1)
                    pe.wait_ge(m_read[1], r[1] + 1)
                tall_group(g + 6 + c, q + 6 + c, lh, ll, 0, 4, 4 * DQ, True, True)

            def mla_ready(i):
                if i % 8 == 0:
                    pe.wait_ge(q_rotated, i // 8 + 1)
                    pe.wait_ge(heads_ready, NT * (i // 8 + 1))
                    fill = q + 5
                    pe.wait_ge(acc_read[fill % 2], acc_reads(fill))

            step = heads("mla", H, DQ, lambda i, t: qn[:, t, i * DQ:(i + 1) * DQ],
                         lambda i, t: kn[:, t, i * DQ:(i + 1) * DQ],
                         lambda i, t: vn[:, t, i * HD:(i + 1) * HD], qkT, probs, pT, mla_ready, lambda j: None)
            for i in range(H + 3):
                step(i)
            turn_o("mla")
            wide_stage(g + 10, q + 10 + H, xh, xl, DK, 0, o_wait("mla"), turn_h("n2", 2))

            ffn("f1", "n2", 2, "n3", 3, with_p=0)

            def ple(name, nname, r, after, r_after):
                g, q, _, _ = PLAN[name]
                fr = PLAN["f1" if name == "p0" else "f3"][3][2]
                wide_stage(g, q, ph, pl, 2, 0, lambda t, k: pe.wait_ge(m_read[2], fr + 1) if t + k == 0 else None,
                           None, True)
                rows_ready(pe, r, 1)
                turn_rows(nname, 1)
                wide_stage(g + 1, q + 2, xh, xl, DK, 0, x_wait(nname), turn_h(after, r_after), True)

            ple("p0", "n3", 3, "n4", 4)
            ffn("f2", "n4", 4, "n5", 5)

            g, q, f, r = PLAN["fox"]
            first_fill("n5", 5, g, q)
            open_acc(q + 1)
            wait_group(g + 2)
            tall_group(g + 2, q + 1, xh, xl, 0, DK, H, True, True)
            for c in range(1, 6):
                open_acc(q + 1 + c)
                for k in range(2):
                    wait_group(g + 1 + 2 * c + k)
                    tall_group(g + 1 + 2 * c + k, q + 1 + c, xh, xl, 4 * k, 4, 512, k == 0, k == 1)
                if c == 1:
                    pe.wait_ge(forget_in, 2)
                    open_m(3, r[3])
                    pe.matmul(M[:, 3, 0:H], tri[:, :], fl[:, 2, 0, :], start=True, stop=True)
                    pe.matmul(M[:, 3, H:2 * H], ones[:, :], fl[:, 2, 0, :], start=True, stop=False)
                    pe.matmul(M[:, 3, H:2 * H], tri[:, :], fl[:, 2, 1, :], start=False,
                              stop=True).then_inc(m_ready[3], 1)

            def fox_ready(i):
                if i == 0:
                    pe.wait_ge(m_read[3], r[3] + 1)
                for c in (0, 2, 4):
                    fill = q + fox_fill(c + i // 8)
                    if i % 8 == 0:
                        pe.wait_ge(acc_read[fill % 2], acc_reads(fill))

            step = heads("fox", H, DF, lambda i, t: qn[:, t, i * DF:(i + 1) * DF],
                         lambda i, t: kn[:, t, i * DF:(i + 1) * DF],
                         lambda i, t: vn[:, t, i * HD:(i + 1) * HD], qkT, probs, pT, fox_ready, lambda j: None)
            for i in range(H + 3):
                step(i)
            turn_o("fox")
            wide_stage(g + 13, q + 7 + H, xh, xl, DK, 0, o_wait("fox"), turn_h("n6", 6))

            ffn("f3", "n6", 6, "n7", 7, with_p=1)
            ple("p1", "n7", 7, "n8", 8)

            g, q, f, r = PLAN["b2"]

            def b2_ready(i):
                if i % H8 == 0:
                    for c in B2_QKV[i // H8]:
                        fill = q + B2_FILL[c]
                        pe.wait_ge(acc_read[fill % 2], acc_reads(fill))

            def qkv_of(n, i, t):
                j = i % H8
                return qkv[:, (i // H8) % 2, n, t, j * HD:(j + 1) * HD]

            step = heads("b2", NH2, HD, lambda i, t: qkv_of(0, i, t), lambda i, t: qkv_of(1, i, t),
                         lambda i, t: qkv_of(2, i, t), qkT2, pr2, pT2, b2_ready, lambda j: None, full=True)
            def turn_fill(fill, rows, back=False):
                open_acc(fill)
                for k in range(4):
                    for t in range(NT):
                        o = (k % 2) * S + t * P
                        dst, src = acc(fill, k // 2)[:, o:o + P], rows[:, t, k * P:(k + 1) * P]
                        if back:
                            mm = pe.matmul(dst, src, flip[:, :], start=True, stop=True)
                        else:
                            mm = pe.transpose(dst, src, ident[:, :])
                mm.then_inc(acc_ready, 1)

            at = 0
            for c in range(len(B2_CHUNKS)):
                if c == 0:
                    first_fill("n8", 8, g, q)
                    continue
                open_acc(q + B2_FILL[c])
                for k in range(2):
                    w = 2 * c + k
                    wait_group(g + w)
                    tall_group(g + w, q + B2_FILL[c], xh, xl, 4 * k, 4, 512, k == 0, k == 1)
                    for _ in range(B2_STEPS[w]):
                        step(at)
                        at += 1
                if c == 10:
                    fill = q + B2_POOL
                    open_acc(fill)
                    pe.wait_ge(b2_small, 16 * 3)
                    for j in range(4):
                        for t in range(NT):
                            mm = pe.matmul(acc(fill, j // 2)[:, (j % 2) * S:(j % 2 + 1) * S],
                                           u[:, t, j * P:(j + 1) * P], bands[:, t, j, :],
                                           start=t == 0, stop=t == NT - 1)
                    mm.then_inc(acc_ready, 1)
                if c == 11:
                    fill = q + B2_MIX
                    open_acc(fill)
                    pe.wait_ge(acc_read[(q + B2_POOL) % 2], acc_reads(q + B2_POOL))
                    for t in range(NT):
                        for j in range(4):
                            mm = pe.matmul(acc(fill, t)[:, j * P:(j + 1) * P], plT[:, j, t * P:(t + 1) * P],
                                           wp[:, j, :], start=True, stop=True)
                    mm.then_inc(acc_ready, 1)
                if c == 13:
                    pe.wait_ge(acc_read[(q + B2_MIX) % 2], acc_reads(q + B2_MIX))
                    turn_fill(q + B2_YAT, s_a)
                if c == 12:
                    fill = q + B2_PERM
                    open_acc(fill)
                    pe.wait_ge(acc_read[(q + B2_FILL[11]) % 2], acc_reads(q + B2_FILL[11]))
                    for t in range(NT):
                        mm = pe.matmul(acc(fill, t), flip[:, :], s_b[:, t, :], start=True, stop=True)
                    mm.then_inc(acc_ready, 1)
                if c == 14:
                    pe.wait_ge(o_done, 1)
                    turn_fill(q + B2_YBT, orev, True)
            wide_stage(g + 32, q + B2_PA, yah, yal, 4, 0,
                       lambda t, k: pe.wait_ge(acc_read[(q + B2_YAT) % 2], acc_reads(q + B2_YAT)) if t + k == 0
                       else None)

            def turn_merged(t):
                pe.wait_ge(mg_done, t + 1)
                turn_rows("b2", t, mg, B2_END)

            wide_stage(g + 34, q + B2_PB, ybh, ybl, 4, 0,
                       lambda t, k: pe.wait_ge(acc_read[(q + B2_YBT) % 2], acc_reads(q + B2_YBT)) if t + k == 0
                       else None, lambda: turn_merged(0), True)

            def merged_wait(t, k):
                if t == 0 and k == 2:
                    turn_merged(1)
                pe.wait_ge(m_read[2 * t + k % 2], B2_END[2 * t + k % 2] + 1)

            wide_stage(g + 36, q + B2_OUT, xh, xl, DK, 0, merged_wait, None, True)

        @block.scalar
        def _(act):
            act.dma_start(ident[:, :], I["c_mats"][0]).then_inc(ident_in, 16)
            act.dma_start(gains[:, :], I["gains"]).then_inc(gains_in, 16)

            done = [0]

            def split(g, i=0):
                s, n = g % RING, columns(g)
                act.wait_ge(raw_in[s], 32 * (g // RING + 1) + 32 * i)
                if g >= RING:
                    act.wait_ge(w_used, g - RING + 1 + RING * i)
                act.activation(wh[:, s, 0:n], raw[:, s, 0:n], ACT.Copy).then_inc(hi_done, 1)

            def split_half(n):
                g = done[0]
                s, w = g % RING, slice(n * GC // 2, (n + 1) * GC // 2)
                act.wait_ge(raw_in[s], 32 * (g // RING + 1))
                act.wait_ge(w_used, g - RING + 1)
                e = act.activation(wh[:, s, w], raw[:, s, w], ACT.Copy)
                if n:
                    e.then_inc(hi_done, 1)
                    done[0] += 1

            def split_to(n):
                for g in range(done[0], min(n, NGROUPS)):
                    split(g)
                done[0] = max(done[0], min(n, NGROUPS))

            def squares(r, t):
                rows_ready(act, r, t)
                act.activation(hn[:, t, :], h[:, t, :], ACT.Square, accum_out=ssq[:, t:t + 1])\
                   .then_inc(sq_done, 1)

            def norm(name, r, before=None, gate=False):
                f, rd = PLAN[name][2:]
                for t in range(NT):
                    for k in range(DK):
                        b = 2 * t + k % 2
                        if r + t == 0 and k == 4:
                            split_to(1)
                        if k < 2:
                            act.wait_ge(m_ready[b], f[b] + 1)
                        else:
                            act.wait_ge(m_read[b], rd[b] + k // 2)
                        c = NORM_GAIN[r] + k
                        act.activation(xh[:, k, t * P:(t + 1) * P], M[:, b, (k // 2) * P:(k // 2 + 1) * P],
                                       ACT.Copy, scale=gains[:, c:c + 1]).then_inc(xh_done, 1)
                    if before and t + 1 < NT:
                        before(t + 1)
                    if not gate:
                        squares(r, t)
                        if t + 1 < NT and r:
                            split_to(done[0] + 1)

            def scaled(r, t):
                act.wait_ge(rstd_done, NT * r + t + 1)
                return rstd[:, t:t + 1]

            def ffn(name, r):
                g0, q0, f0, _ = PLAN[name]

                def silus(c, i=0):
                    q, g = q0 + c, g0 + 2 * c + 1
                    for t in range(NT):
                        tile_ready(act, q, t, g, i, 2)
                        if c == 0:
                            scaled(r, t)
                        act.activation(sg[:, c % 2, t, :], acc(q, t)[:, 0:256], ACT.Silu,
                                       scale=rstd[:, t:t + 1]).then_inc(silu_done, 1)

                def round_a(c, i=0):
                    b = c % 2
                    act.wait_ge(m_ready[b], f0[b] + c // 2 + 1 + i)
                    act.activation(ah[:, bass.ds(i * 4 + 2 * c, 2), :],
                                   M[:, b, :].rearrange("p (k n) -> p k n", k=2), ACT.Copy).then_inc(ah_done, 1)

                peel = 3 if g0 == 0 else 1
                for c in range(peel):
                    split_to(g0 + 2 * c + 3)
                    if c:
                        round_a(c - 1)
                    split_to(g0 + 2 * c + 4)
                    silus(c)
                    if g0 == 0 and c == 1:
                        act.wait_ge(angles, 1)
                        act.activation(cs[:, :, :, :], rc[:, :, :, :], ACT.Sin).then_inc(sines, 1)
                with act.Fori(0, (FCH - peel) // 2) as i:
                    for c in range(peel, peel + 2):
                        split(g0 + 2 * c + 2, i)
                        round_a(c - 1, i)
                        split(g0 + 2 * c + 3, i)
                        silus(c, i)
                done[0] = g0 + 2 * FCH + 2
                split_to(g0 + 2 * FCH + 3)
                round_a(FCH - 1)
                if name in ("f1", "f3"):
                    act.wait_ge(m_ready[2], f0[2] + 1)
                    act.activation(ph[:, :, :], M[:, 2, :].rearrange("p (k n) -> p k n", k=2), ACT.Copy)\
                       .then_inc(ph_done, 1)
                split_to(g0 + 3 * FCH + 2)

            act.wait_ge(gains_in, 16)
            act.activation(rs[:, 0, 0:1], gains[:, 0:1], ACT.Copy)
            norm("n0", 0, lambda t: split_to(2))
            ffn("f0", 0)
            norm("n1", 1)
            act.wait_ge(m_read[3], PLAN["n1"][3][3])
            act.dma_start(scratch[:, :].rearrange("(g h) n -> h g n", g=G3), tsb[:, :, :]).then_inc(table_out, 16)

            g, q, f, r = PLAN["mla"]
            split_to(g + 4)
            for t in range(NT):
                tile_ready(act, q, t, g + 1)
                act.activation(lat[:, t, QR:QR + KVR], acc(q, t)[:, 0:KVR], ACT.Square, scale=scaled(1, t),
                               accum_out=lss[:, 1, t:t + 1]).then_inc(lat_sq, 1)
                act.activation(kpr[:, t, :], acc(q, t)[:, KVR:KVR + ROPE], ACT.Square, scale=rstd[:, t:t + 1],
                               accum_out=kss[:, t:t + 1]).then_inc(lat_sq, 1)

            def round_latents(ks):
                for k in ks:
                    act.wait_ge(m_ready[k // 2], f[k // 2] + 1)
                    c = G_QLAT + k
                    act.activation(lh[:, k, :], M[:, k // 2, (k % 2) * S:(k % 2 + 1) * S], ACT.Copy,
                                   scale=gains[:, c:c + 1]).then_inc(lh_done, 1)

            split_to(g + 5)
            round_latents(range(4, 6))
            split_to(g + 6)
            for t in range(NT):
                tile_ready(act, q + 1, t, g + 3)
                act.activation(lat[:, t, 0:QR], acc(q + 1, t), ACT.Square, scale=rstd[:, t:t + 1],
                               accum_out=lss[:, 0, t:t + 1]).then_inc(lat_sq, 1)
            split_to(g + 7)
            kn4 = kn.rearrange("p t (h d) -> p t h d", d=DQ)
            for c in range(2):
                for n in range(2):
                    fill = q + 2 + 2 * c + n
                    tile_ready(act, fill, 0, g + 4 + c)
                    if c == 0:
                        act.wait_ge(acc_read[fill % 2], acc_reads(fill - 2))
                    act.wait_ge(lat_rstd, 1)
                    copy_kv(nc.scalar, fill, 0, 2 * c + n)
                if c == 0:
                    split_to(g + 8)
                    round_latents(range(4))
                else:
                    split_to(g + 9)
                act.wait_ge(table_out, 16)
                for t in range(NT):
                    for n in range(2):
                        fill = q + 2 + 2 * c + n
                        act.wait_ge(acc_read[fill % 2], acc_reads(fill))
                    act.activation(sqb[:, t, 512 * c:512 * c + 512].rearrange("p (h d) -> p h d", d=NOPE),
                                   kn4[:, t, 8 * c:8 * c + 8, 0:NOPE], ACT.Square).then_inc(heads_sq, 1)

            def square_queries(c):
                w = slice(768 * c, 768 * c + 768)
                for t in range(NT):
                    for fill in (PLAN["mla"][1] + 6 + 2 * c, PLAN["mla"][1] + 7 + 2 * c):
                        act.wait_ge(acc_read[fill % 2], acc_reads(fill))
                    act.wait_ge(heads_ss, 2 * NT)
                    act.activation(sqb[:, t, w], qn[:, t, w], ACT.Square).then_inc(heads_sq, 1)

            for c in range(4):
                fill = q + 6 + c
                tile_ready(act, fill, 0, g + 6 + c)
                act.wait_ge(lat_rstd, 2 + 1)
                act.activation(qn[:, 0, 384 * c:384 * c + 384], acc(fill, 0)[:, 0:384], ACT.Copy,
                               scale=lrs[:, 0, 0:1]).then_inc(acc_read[fill % 2], 1)
                if c == 1:
                    square_queries(0)
                split_to(g + 10 + c // 2)

            def heads(name, nh, dk, col):
                f, _ = HEADS[name]
                first = 0 if name == "mla" else H
                sq = PLAN[name][1] + S_FILL[name]

                def step(i):
                    if i < nh:
                        tb, tn = i % 2, i // 2
                        act.wait_ge(m_ready[tb], f[tb] + tn + 1)
                        if i >= 2:
                            act.wait_ge(acc_ready, sq + i - 1)
                        act.activation(qkT[0:dk, i % 2, 0:S], M[0:dk, tb, 0:S], ACT.Copy,
                                       scale=headg[0:dk, col:col + 1]).then_inc(m_read[tb], 1)
                    j = i - 1
                    if 0 <= j < nh:
                        act.wait_ge(max_done, first + j + 1)
                        if j >= 2:
                            act.wait_ge(m_ready[2], f[2] + j - 1)
                        for t, (a, b) in enumerate(((0, P), (P, 3 * P))):
                            act.activation(probs[:, j % 2, a:b], acc(sq + j, 0)[:, a:b], ACT.Exp,
                                           bias=nmx[:, t, j:j + 1],
                                           scale=hrs[:, t, j:j + 1] if name == "mla" else 1.0,
                                           accum_out=rs[:, t, j:j + 1]).then_inc(acc_read[(sq + j) % 2], 1)
                return step

            def round_rows(fills):
                for b in range(4):
                    act.wait_ge(m_ready[b], fills[b] + 1)
                    t = b // 2
                    act.activation(xh[:, b % 2::2, t * P:(t + 1) * P], M[:, b, :].rearrange("p (k n) -> p k n", k=4),
                                   ACT.Copy).then_inc(oh_done, 1)

            step = heads("mla", H, DQ, 0)
            for i in range(H + 1):
                step(i)
                if i == 0:
                    square_queries(1)
                if 1 <= i < 7:
                    split_half((i + 1) % 2)
            round_rows(OT_FILLS["mla"])
            split_to(g + 16)
            norm("n2", 2)
            ffn("f1", 2)

            def ple(name, nname, r, after, r_after):
                g, q, _, _ = PLAN[name]

                def sigmoids(t):
                    for n in range(2):
                        fill = q + 2 + n
                        tile_ready(act, fill, t, g + 4)
                        act.activation(gate[:, t, 512 * n:512 * n + 512], acc(fill, t), ACT.Sigmoid,
                                       scale=scaled(r, t)).then_inc(acc_read[fill % 2], 1)

                def project(t):
                    for t in range(NT):
                        split_to(g + 3 + t)
                        for n in range(2):
                            tile_ready(act, q + n, t, g)
                            if t == 0:
                                act.wait_ge(acc_read[(q + n) % 2], acc_reads(q + n - 2))
                            act.activation(pp[:, t, 512 * n:512 * n + 512], acc(q + n, t), ACT.Copy)\
                               .then_inc(acc_read[(q + n) % 2], 1)

                norm(nname, r, project, True)
                split_to(g + 5)
                for t in range(NT):
                    squares(r, t)
                sigmoids(0)
                split_to(g + 7)
                norm(after, r_after, sigmoids)

            ple("p0", "n3", 3, "n4", 4)
            ffn("f2", 4)

            norm("n5", 5)
            g, q, f, r = PLAN["fox"]
            split_to(g + 4)
            for c in range(6):
                e = g + 1 if c == 0 else g + 2 + 2 * c
                fill = q + fox_fill(c)
                if c:
                    split_to(e + 3)
                for t in range(NT):
                    if c == 0 and t:
                        split_to(g + 5)
                    tile_ready(act, fill, t, e)
                    if c < 4:
                        if c >= 2:
                            act.wait_ge(heads_ss, 8 + 2 * (c - 2) + t + 1)
                        act.activation(sqb[:, t, 512 * (c % 2):512 * (c % 2) + 512], acc(fill, t), ACT.Square,
                                       scale=scaled(5, t)).then_inc(heads_sq, 1)
                    else:
                        act.activation(vn[:, t, 512 * (c - 4):512 * (c - 3)], acc(fill, t), ACT.Copy,
                                       scale=rstd[:, t:t + 1]).then_inc(acc_read[fill % 2], 1)
                    if c == 0:
                        if t == 0:
                            act.wait_ge(acc_read[q % 2], acc_reads(q - 2))
                        act.activation(qn[:, t, 0:8 * DF].rearrange("p (h d) -> p h d", d=DF)[:, :, 0:HD],
                                       acc(q, t).rearrange("p (h d) -> p h d", d=HD), ACT.Copy)\
                           .then_inc(acc_read[q % 2], 1)
                if c == 0:
                    act.wait_ge(acc_read[(q + 1) % 2], acc_reads(q + 1))
                    act.activation(fl[:, 1, :, :], fl[:, 0, :, :], ACT.Abs).then_inc(forget_exp, 1)
                    act.wait_ge(forget_exp, 1)
                    act.activation(fl[:, 1, :, :], fl[:, 1, :, :], ACT.Exp, scale=-1.0).then_inc(forget_exp, 1)
                    act.wait_ge(forget_exp, 2)
                    act.activation(fl[:, 1, :, :], fl[:, 1, :, :], ACT.Ln, bias=1.0).then_inc(forget_exp, 1)
            step = heads("fox", H, DF, 2)
            for i in range(H + 1):
                step(i)
                if 1 <= i < 5:
                    split_half((i + 1) % 2)
            round_rows(OT_FILLS["fox"])
            split_to(g + 19)
            norm("n6", 6)
            ffn("f3", 6)
            ple("p1", "n7", 7, "n8", 8)

            g, q, f, r = PLAN["b2"]
            hf = HEADS["b2"][0]

            def b2_step(i):
                if i < NH2:
                    act.wait_ge(m_ready[0], hf[0] + i + 1)
                    if i >= 2:
                        act.wait_ge(m_ready[1], hf[1] + i - 1)
                    act.activation(qkT2[:, i % 2, 0:S], M[0:HD, 0, 0:S], ACT.Copy, scale=HD ** -0.5)\
                       .then_inc(m_read[0], 1)
                j = i - 1
                if 0 <= j < NH2:
                    act.wait_ge(max_done, 2 * H + j + 1)
                    for t in range(NT):
                        e = act.activation(pr2[:, t * S:(t + 1) * S], pr2[:, t * S:(t + 1) * S], ACT.Exp,
                                           bias=nmx[:, t, j:j + 1], accum_out=rs[:, t, j:j + 1])
                    e.then_inc(exp_done, 1)

            at = 0
            for c, (what, j) in enumerate(B2_CHUNKS):
                fill = q + B2_FILL[c]
                for k in range(2):
                    w = 2 * c + k
                    split_to(g + w + 3)
                    gates_first = k == 1 and what in ("a_gate", "b_gp")
                    if not gates_first:
                        for _ in range(B2_STEPS[w]):
                            b2_step(at)
                            at += 1
                    if w == B2_COMBINE:
                        act.wait_ge(combine_in, 1)
                        act.activation(cmb[:, 2, :], cmb[:, 1, :], ACT.Exp).then_inc(combine_exp, 1)
                    if k == 1:
                        for t in range(NT):
                            if what in ("q", "v"):
                                tile_ready(act, fill, t, g + w)
                                act.activation(qkv[:, j % 2, 0 if what == "q" else 2, t, :], acc(fill, t),
                                               ACT.Copy, scale=scaled(8, t)).then_inc(acc_read[fill % 2], 1)
                            elif what in ("a_gate", "b_gp"):
                                tile_ready(act, fill, t, g + w)
                                act.activation((s_a if what == "a_gate" else s_b)[:, t, :], acc(fill, t),
                                               ACT.Silu, scale=rstd[:, t:t + 1]).then_inc(acc_read[fill % 2], 1)
                            elif what == "g":
                                act.wait_ge(acc_read[fill % 2], acc_reads(fill) - 1 + t)
                                part = gts[:, t, 512 * j:512 * j + 512]
                                act.activation(part, part, ACT.Sigmoid).then_inc(gate_done, 1)
                    if gates_first:
                        for _ in range(B2_STEPS[w]):
                            b2_step(at)
                            at += 1
                if c == 10:
                    pf = q + B2_POOL
                    for t in range(NT):
                        tile_ready(act, pf, t, None)
                        act.activation(plT[:, 2 * t:2 * t + 2, :],
                                       acc(pf, t).rearrange("p (k n) -> p k n", k=2), ACT.Copy)\
                           .then_inc(acc_read[pf % 2], 1)
                if c == 12:
                    pf = q + B2_PERM
                    for t in range(NT):
                        tile_ready(act, pf, t, None)
                        act.activation(s_b[:, t, :], acc(pf, t), ACT.Copy).then_inc(acc_read[pf % 2], 1)
                if c == 13:
                    pf = q + B2_YAT
                    for k in range(4):
                        act.wait_ge(acc_ready, pf + 1)
                        act.activation(yah[:, k, :], acc(pf, k // 2)[:, (k % 2) * S:(k % 2 + 1) * S], ACT.Copy,
                                       scale=gains[:, G_POOL + k:G_POOL + k + 1]).then_inc(oh_done, 1)
                if c == 14:
                    pf = q + B2_YBT
                    for b in range(2):
                        act.wait_ge(acc_ready, pf + 1)
                        act.activation(ybh[:, 2 * b:2 * b + 2, :], acc(pf, b).rearrange("p (k n) -> p k n", k=2),
                                       ACT.Copy).then_inc(oh_done, 1)
            split_to(g + 39)
            for b in range(4):
                if b == 2:
                    split_to(g + 40)
                act.wait_ge(m_ready[b], hf[b] + NH2 + 1)
                t = b // 2
                act.activation(xh[:, b % 2::2, t * P:(t + 1) * P], M[:, b, :].rearrange("p (k n) -> p k n", k=4),
                               ACT.Copy).then_inc(oh_done, 1)
            for t in range(NT):
                squares(9, t)

        @block.vector
        def _(dve):
            done = [0]
            steps = [0]

            def link(ins):
                steps[0] += 1
                ins.then_inc(v_step, 1)
                dve.wait_ge(v_step, steps[0])

            def split(g, i=0):
                s, n = g % RING, columns(g)
                dve.wait_ge(hi_done, g + 1 + RING * i)
                dve.tensor_tensor(wl[:, s, 0:n], raw[:, s, 0:n], wh[:, s, 0:n].bitcast(F32), ALU.subtract)\
                   .then_inc(lo_done, 1)

            def split_quarter(n):
                g = done[0]
                s, w = g % RING, slice(n * GC // 4, (n + 1) * GC // 4)
                dve.wait_ge(hi_done, g + 1)
                e = dve.tensor_tensor(wl[:, s, w], raw[:, s, w], wh[:, s, w].bitcast(F32), ALU.subtract)
                if n == 3:
                    e.then_inc(lo_done, 1)
                    done[0] += 1

            def split_to(n):
                for g in range(done[0], min(n, NGROUPS)):
                    split(g)
                done[0] = max(done[0], min(n, NGROUPS))

            def rest(name, r, t):
                for k in range(DK):
                    b = 2 * t + k % 2
                    if r + t == 0 and k == 4:
                        split_to(1)
                    dve.wait_ge(xh_done, NT * DK * r + DK * t + k + 1)
                    c = NORM_GAIN[r] + k
                    dve.scalar_tensor_tensor(xl[:, k, t * P:(t + 1) * P], M[:, b, (k // 2) * P:(k // 2 + 1) * P],
                                             gains[:, c:c + 1], xh[:, k, t * P:(t + 1) * P].bitcast(F32),
                                             ALU.mult, ALU.subtract).then_inc(m_read[b], 1)

            def scaled(r, t):
                dve.wait_ge(rstd_done, NT * r + t + 1)
                return rstd[:, t:t + 1]

            def pair(ap):
                return ap.rearrange("p (k n) -> p k n", k=2)

            def angles_reduced():
                dve.wait_ge(small_in, 16 * SMALL)
                dve.memset(ones[:, :], 1.0).then_inc(v_step, 1)
                steps[0] += 1
                link(dve.tensor_copy(posf[:, :], posi[:, :]))
                for t in range(NT):
                    link(dve.tensor_scalar(ang[:, t, :], freq[:, :], posf[:, t:t + 1], None, ALU.mult))
                big = 1.5 * 2.0 ** 23
                link(dve.tensor_scalar(turns[:, :, :], ang[:, :, :], 1.0 / (2.0 * np.pi), None, ALU.mult))
                link(dve.tensor_scalar(turns[:, :, :], turns[:, :, :], big, None, ALU.add))
                link(dve.tensor_scalar(turns[:, :, :], turns[:, :, :], -big, None, ALU.add))
                c1 = 6.28125
                c2 = float(np.float32(np.round((2 * np.pi - c1) * 2.0 ** 20) / 2.0 ** 20))
                c3 = float(np.float32(2 * np.pi - c1 - c2))
                for part in (c1, c2, c3):
                    link(dve.scalar_tensor_tensor(ang[:, :, :], turns[:, :, :], -part, ang[:, :, :],
                                                  ALU.mult, ALU.add))
                link(dve.tensor_scalar(rc[:, 0, :, :], ang[:, :, :], float(np.pi / 2), None, ALU.add))
                link(dve.tensor_scalar(wrap[:, :, :], rc[:, 0, :, :], float(np.pi), -2.0 * float(np.pi),
                                       ALU.is_gt, ALU.mult))
                link(dve.tensor_tensor(rc[:, 0, :, :], rc[:, 0, :, :], wrap[:, :, :], ALU.add))
                lim = float(np.nextafter(np.float32(np.pi), np.float32(0)))
                link(dve.tensor_scalar(rc[:, 0, :, :], rc[:, 0, :, :], lim, -lim, ALU.min, ALU.max))
                dve.tensor_scalar(rc[:, 1, :, :], ang[:, :, :], lim, -lim, ALU.min, ALU.max).then_inc(angles, 1)

            def head_constants():
                dve.memset(headg[:, 1:4], 1.0).then_inc(v_step, 1)
                link(dve.memset(headg[:, 0:1], DQ ** -0.5))
                steps[0] += 1
                dve.wait_ge(v_step, steps[0])
                for n, scale in enumerate((DQ ** -0.5, 1.0, HD ** -0.5, 1.0)):
                    link(dve.tensor_scalar(headg[0:HD, n:n + 1], hraw[:, n:n + 1], scale, None, ALU.mult))
                link(dve.tensor_copy(identb[:, :], ident[:, :]))
                dve.memset(causal[:, 0:P], 0.0)
                link(dve.tensor_copy(causal[:, P:2 * P], causal_f[:, :]))
                link(dve.memset(rb[32:33, :], NEG))

            def rope_tables():
                dve.wait_ge(sines, 1)
                for n in range(2):
                    for t in range(NT):
                        for c, (half, fn) in enumerate(((0, 0), (1, 1), (0, 1), (1, 0))):
                            link(dve.tensor_tensor(tab[:, n, t, c, :], rgain[:, n, 16 * half:16 * half + 16],
                                                   cs[:, fn, t, :], ALU.mult))
                dve.tensor_copy(mxp[:, 0, :], posf[:, :]).then_inc(const_ready, 1)

            def residual(q, g, scale, t):
                for n in range(2):
                    tile_ready(dve, q + n, t, g)
                    part = h[:, t, 512 * n:512 * n + 512]
                    dve.scalar_tensor_tensor(part, acc(q + n, t), scale, part, ALU.mult, ALU.add)\
                       .then_inc(acc_read[(q + n) % 2], 1)

            def next_norm(name, r, q, g, scale, more=1):
                for t in range(NT):
                    residual(q, g, scale, t)
                    if t:
                        split_to(done[0] + more)
                    rest(name, r, t)

            def ffn(name, r, after):
                g0, q0, f0, _ = PLAN[name]
                base = FIRST_SILU[name] * FCH

                def gated(c, i=0):
                    q = q0 + c
                    for t in range(NT):
                        dve.wait_ge(silu_done, NT * (base + c) + t + 1 + 4 * i)
                        dve.scalar_tensor_tensor(a_n[:, c % 2, t, :], acc(q, t)[:, 256:512], rstd[:, t:t + 1],
                                                 sg[:, c % 2, t, :], ALU.mult, ALU.mult)\
                           .then_inc(acc_read[q % 2], 1)

                def rest_a(c, i=0):
                    b = c % 2
                    dve.wait_ge(ah_done, base + c + 1 + 2 * i)
                    dve.tensor_tensor(al[:, bass.ds(i * 4 + 2 * c, 2), :], pair(M[:, b, :]),
                                      ah[:, bass.ds(i * 4 + 2 * c, 2), :].bitcast(F32), ALU.subtract)\
                       .then_inc(m_read[b], 1)

                peel = 3 if g0 == 0 else 1
                for c in range(peel):
                    split_to(g0 + 2 * c + 3)
                    if c:
                        rest_a(c - 1)
                    split_to(g0 + 2 * c + 4)
                    gated(c)
                    if g0 == 0:
                        (angles_reduced, head_constants, rope_tables)[c]()
                with dve.Fori(0, (FCH - peel) // 2) as i:
                    for c in range(peel, peel + 2):
                        split(g0 + 2 * c + 2, i)
                        rest_a(c - 1, i)
                        split(g0 + 2 * c + 3, i)
                        gated(c, i)
                done[0] = g0 + 2 * FCH + 2
                split_to(g0 + 2 * FCH + 3)
                rest_a(FCH - 1)
                if name in ("f1", "f3"):
                    dve.wait_ge(ph_done, 1 if name == "f1" else 2)
                    dve.tensor_tensor(pl[:, :, :], pair(M[:, 2, :]), ph[:, :, :].bitcast(F32), ALU.subtract)\
                       .then_inc(m_read[2], 1)
                if g0 == 0:
                    for j, c in enumerate(TABLE_AT):
                        split_to(g0 + 2 * FCH + c + 3)
                        dve.wait_ge(m_ready[3], f0[3] + j + 1)
                        dve.tensor_copy(tsb[:, j, :], M[0:H8, 3, :]).then_inc(m_read[3], 1)
                split_to(g0 + 3 * FCH + 2)
                next_norm(after, r + 1, q0 + FCH, g0 + 3 * FCH - 1, 0.5, {"n1": 0, "n3": 2, "n7": 2}.get(after, 1))

            dve.wait_ge(gains_in, 16)
            rest("n0", 0, 0)
            split_to(2)
            rest("n0", 0, 1)

            ffn("f0", 0, "n1")

            g, q, f, r = PLAN["mla"]
            split_to(g + 4)
            for t in range(NT):
                dve.wait_ge(lat_sq, 2 * t + 2)
                dve.tensor_scalar(kpe[:, t, :], acc(q, t)[:, KVR:KVR + ROPE], scaled(1, t), None, ALU.mult)
                dve.tensor_scalar(lat[:, t, QR:QR + KVR], acc(q, t)[:, 0:KVR], rstd[:, t:t + 1], None,
                                  ALU.mult).then_inc(acc_read[q % 2], 1)

            def rest_latents(ks):
                for k in ks:
                    if k % 2 == 0:
                        dve.wait_ge(lh_done, (k - 4) % 6 + 2)
                    c = G_QLAT + k
                    e = dve.scalar_tensor_tensor(ll[:, k, :], M[:, k // 2, (k % 2) * S:(k % 2 + 1) * S],
                                                 gains[:, c:c + 1], lh[:, k, :].bitcast(F32),
                                                 ALU.mult, ALU.subtract)
                    if k % 2:
                        e.then_inc(m_read[k // 2], 1)

            def rotate(eng, x1, x2, table, tmp, ln):
                for n, (x, c) in enumerate(((x1, 0), (x2, 1), (x1, 2), (x2, 3))):
                    ln(eng.tensor_tensor(tmp[n], x, table[c], ALU.mult))
                ln(eng.tensor_tensor(x1, tmp[0], tmp[1], ALU.subtract))
                ln(eng.tensor_tensor(x2, tmp[2], tmp[3], ALU.add))

            split_to(g + 5)
            rest_latents(range(4, 6))
            split_to(g + 6)
            for t in range(NT):
                dve.wait_ge(lat_sq, 2 * NT + t + 1)
                dve.tensor_scalar(lat[:, t, 0:QR], acc(q + 1, t), rstd[:, t:t + 1], None, ALU.mult)\
                   .then_inc(acc_read[(q + 1) % 2], 1)
            split_to(g + 7)
            dve.wait_ge(acc_read[q % 2], acc_reads(q))
            for t in range(NT):
                rotate(dve, kpe[:, t, 0:16], kpe[:, t, 16:32], [tab[:, 1, t, c, :] for c in range(4)],
                       [kpr[:, 0, 0:16], kpr[:, 0, 16:32], kpr[:, 1, 0:16], kpr[:, 1, 16:32]], link)
            heads3 = lambda ap, d: ap.rearrange("p (h d) -> p h d", d=d)

            def sum_keys(c):
                for t in range(NT):
                    dve.wait_ge(heads_sq, NT * c + t + 1)
                    o = hss[:, 2 + t, 8 * c:8 * c + 8]
                    link(dve.tensor_reduce(o, heads3(sqb[:, t, 512 * c:512 * c + 512], NOPE), AX, ALU.add))
                    dve.tensor_scalar(o, o, kss[:, t:t + 1], None, ALU.add).then_inc(heads_ss, 1)

            def sum_queries(c):
                for t in range(NT):
                    dve.wait_ge(heads_sq, 2 * NT + NT * c + t + 1)
                    dve.tensor_reduce(hss[:, t, 8 * c:8 * c + 8],
                                      heads3(sqb[:, t, 768 * c:768 * c + 768], DQ),
                                      AX, ALU.add).then_inc(heads_ss, 1)

            def scale_keys(c):
                for t in range(NT):
                    dve.wait_ge(heads_rstd, NT * c + t + 1)
                    kv = heads3(kn[:, t, :], DQ)[:, 8 * c:8 * c + 8]
                    by = hrs[:, 2 + t, 8 * c:8 * c + 8].unsqueeze(2)
                    dve.tensor_tensor(kv[:, :, 0:NOPE], kv[:, :, 0:NOPE], by.to_broadcast([P, 8, NOPE]), ALU.mult)
                    dve.tensor_tensor(kv[:, :, NOPE:DQ], kpe[:, t, :].unsqueeze(1).to_broadcast([P, 8, ROPE]),
                                      by.to_broadcast([P, 8, ROPE]), ALU.mult).then_inc(heads_ready, 1)

            for c in range(2):
                for n in range(2):
                    fill = q + 2 + 2 * c + n
                    tile_ready(dve, fill, 1, g + 4 + c)
                    dve.wait_ge(lat_rstd, 2)
                    copy_kv(nc.vector, fill, 1, 2 * c + n)
                if c == 0:
                    rest_latents(range(4))
                split_to(g + 8 + c)
                sum_keys(c)
                if c:
                    scale_keys(0)
            for c in range(4):
                fill = q + 6 + c
                tile_ready(dve, fill, 1, g + 6 + c)
                dve.wait_ge(lat_rstd, 2 + 2)
                dve.tensor_scalar(qn[:, 1, 384 * c:384 * c + 384], acc(fill, 1)[:, 0:384], lrs[:, 0, 1:2], None,
                                  ALU.mult).then_inc(acc_read[fill % 2], 1)
                if c == 0:
                    scale_keys(1)
                if c == 1:
                    sum_queries(0)
                split_to(g + 10 + c // 2)

            def heads(name, nh, dk, col):
                f, r = HEADS[name]
                sq = PLAN[name][1] + S_FILL[name]

                def step(i):
                    j = i - 1
                    if 0 <= j < nh:
                        dve.wait_ge(acc_ready, sq + j + 1)
                        sc = acc(sq + j, 0)
                        if name == "mla":
                            mx = mxp[:, j % 2, :]
                            dve.tensor_reduce(mx[:, 0:1], sc[:, 0:P], AX, ALU.max, negate=True)
                            link(dve.tensor_reduce(mx[:, 1:2], sc[:, P:3 * P], AX, ALU.max, negate=True))
                            if j % 8 == 0:
                                dve.wait_ge(heads_rstd, 2 * NT + NT * (j // 8) + NT)
                            dve.tensor_tensor(nmx[:, :, j], mx, hrs[:, 0:NT, j], ALU.mult).then_inc(max_done, 1)
                        else:
                            dve.tensor_reduce(nmx[:, 0, j:j + 1], sc[:, 0:P], AX, ALU.max, negate=True)
                            dve.tensor_reduce(nmx[:, 1, j:j + 1], sc[:, P:3 * P], AX, ALU.max, negate=True)\
                               .then_inc(max_done, 1)
                    if i < nh:
                        tb, tn = i % 2, i // 2
                        dve.wait_ge(m_ready[tb], f[tb] + tn + 1)
                        if i >= 2:
                            dve.wait_ge(acc_ready, sq + i - 1)
                        dve.wait_ge(m_read[tb], r[tb] + 2 * tn + 1)
                        dve.tensor_scalar(qkT[0:dk, i % 2, S:2 * S], M[0:dk, tb, S:2 * S],
                                          headg[0:dk, col:col + 1], None, ALU.mult).then_inc(m_read[tb], 1)
                    j = i - 2
                    if 0 <= j < nh:
                        dve.wait_ge(m_ready[2], f[2] + j + 1)
                        if j >= 2:
                            dve.wait_ge(m_ready[3], f[3] + j - 1)
                        dve.tensor_copy(pT[:, j % 2, :], M[:, 2, 0:3 * P]).then_inc(m_read[2], 1)
                        dve.wait_ge(acc_read[(sq + j) % 2], acc_reads(sq + j))
                        dve.reciprocal(rin[:, :, j:j + 1], rs[:, :, j:j + 1]).then_inc(rin_done, 1)
                    j = i - 3
                    if 0 <= j < nh:
                        dve.wait_ge(m_ready[3], f[3] + j + 1)
                        dve.wait_ge(rin_done, (0 if name == "mla" else H) + j + 1)
                        dve.tensor_tensor(hn[:, :, j * HD:(j + 1) * HD],
                                          M[:, 3, 0:2 * HD].rearrange("p (t d) -> p t d", t=NT),
                                          rin[:, :, j:j + 1].to_broadcast([P, NT, HD]), ALU.mult)\
                           .then_inc(m_read[3], 1)
                return step

            def rest_rows(done):
                for b in range(4):
                    t = b // 2
                    dve.wait_ge(oh_done, done + b + 1)
                    dve.tensor_tensor(xl[:, b % 2::2, t * P:(t + 1) * P],
                                      M[:, b, :].rearrange("p (k n) -> p k n", k=4),
                                      xh[:, b % 2::2, t * P:(t + 1) * P].bitcast(F32), ALU.subtract)\
                       .then_inc(m_read[b], 1)

            def attention_out(name, step, g, q, o, r, nname):
                first = done[0]
                for i in range(H + 3):
                    step(i)
                    if 4 <= i < 4 * (g + o + 4 - first + 1):
                        split_quarter(i % 4)
                    if i == 1 and name == "mla":
                        sum_queries(1)
                rest_rows(OH[name])
                residual(q, g + o + 3, 1.0, 0)
                split_to(g + o + 6)
                rest(nname, r, 0)
                residual(q, g + o + 3, 1.0, 1)
                split_to(done[0] + 1)
                rest(nname, r, 1)

            attention_out("mla", heads("mla", H, DQ, 1), g, q + 10 + H, 10, 2, "n2")
            ffn("f1", 2, "n3")

            def ple(name, nname, r, after):
                g, q, _, _ = PLAN[name]

                def embed(t):
                    for n in range(2):
                        fill = q + 2 + n
                        dve.wait_ge(acc_read[fill % 2], acc_reads(fill) - 1 + t)
                        dve.wait_ge(acc_read[(q + n) % 2], acc_reads(q + n))
                        cols = slice(512 * n, 512 * n + 512)
                        link(dve.tensor_tensor(gate[:, t, cols], gate[:, t, cols], pp[:, t, cols], ALU.mult))
                        e = dve.tensor_tensor(h[:, t, cols], h[:, t, cols], gate[:, t, cols], ALU.add)
                        if n:
                            e.then_inc(h_added, 1)

                split_to(g + 5)
                embed(0)
                split_to(g + 7)
                rest(after, r + 1, 0)
                embed(1)
                split_to(done[0] + 1)
                rest(after, r + 1, 1)

            ple("p0", "n3", 3, "n4")
            ffn("f2", 4, "n5")

            g, q, f, r = PLAN["fox"]
            split_to(g + 4)

            def sum_heads(c):
                for t in range(NT):
                    dve.wait_ge(heads_sq, 8 + 2 * c + t + 1)
                    dve.tensor_reduce(hss[:, t, 8 * (c % 2):8 * (c % 2) + 8],
                                      heads3(sqb[:, t, 512 * (c % 2):512 * (c % 2) + 512], HD), AX, ALU.add)\
                       .then_inc(heads_ss, 1)

            def scale_heads(c):
                dst, fill = (qf, kf)[c // 2], q + fox_fill(c)
                if c == 0:
                    dve.wait_ge(acc_read[fill % 2], acc_reads(fill))
                for t in range(NT):
                    dve.wait_ge(heads_rstd, 8 + 2 * c + t + 1)
                    o = dst[:, t, 8 * (c % 2):8 * (c % 2) + 8, 0:HD]
                    e = dve.tensor_tensor(o, o if c == 0 else heads3(acc(fill, t), HD),
                                          hrs[:, t, 8 * (c % 2):8 * (c % 2) + 8].unsqueeze(2).to_broadcast([P, 8, HD]),
                                          ALU.mult)
                    if c:
                        e.then_inc(acc_read[fill % 2], 1)

            qf = qn[:, :, 0:H * DF].rearrange("p t (h d) -> p t h d", d=DF)
            kf = kn[:, :, 0:H * DF].rearrange("p t (h d) -> p t h d", d=DF)
            split_to(g + 5)
            sum_heads(0)
            for t in range(NT):
                tile_ready(dve, q + 1, t, g + 2)
                dve.scalar_tensor_tensor(fl[:, 0, t, :], acc(q + 1, t)[:, 0:H], scaled(5, t), bf[:, :],
                                         ALU.mult, ALU.add).then_inc(acc_read[(q + 1) % 2], 1)
            scale_heads(0)
            dve.wait_ge(forget_exp, 3)
            for t in range(NT):
                dve.scalar_tensor_tensor(fl[:, 2, t, :], fl[:, 0, t, :], 0.0, fl[:, 1, t, :],
                                         ALU.min, ALU.subtract).then_inc(forget_in, 1)
            for c in range(1, 4):
                e = g + 2 + 2 * c
                split_to(e + 2)
                sum_heads(c)
                split_to(e + 3)
                scale_heads(c)
                if c == 1:
                    dve.wait_ge(m_ready[3], f[3] + 1)
                    dec = M[:, 3, 0:2 * H].rearrange("p (t h) -> p t h", t=NT)
                    dve.memset(qf[:, :, :, HD + 1], 1.0)
                    dve.memset(kf[:, :, :, HD], 1.0)
                    dve.tensor_copy(qf[:, :, :, HD], dec)
                    dve.tensor_scalar(kf[:, :, :, HD + 1], dec, -1.0, None, ALU.mult).then_inc(m_read[3], 1)
            for c in range(4, 6):
                split_to(g + 2 + 2 * c + 3)
            attention_out("fox", heads("fox", H, DF, 3), g, q + 7 + H, 13, 6, "n6")
            ffn("f3", 6, "n7")
            ple("p1", "n7", 7, "n8")

            g, q, _, _ = PLAN["b2"]
            hf, hr = HEADS["b2"]

            def b2_step(i):
                if i < NH2:
                    dve.wait_ge(m_ready[0], hf[0] + i + 1)
                    if i >= 2:
                        dve.wait_ge(m_ready[1], hf[1] + i - 1)
                    dve.wait_ge(m_read[0], hr[0] + 2 * i + 1)
                    dve.tensor_copy(qkT2[:, i % 2, S:2 * S], M[0:HD, 0, S:2 * S]).then_inc(m_read[0], 1)
                j = i - 1
                if 0 <= j < NH2:
                    dve.wait_ge(m_ready[1], hf[1] + j + 1)
                    dve.wait_ge(win_in[j % 2], 16 * (j // 2 + 1))
                    if j:
                        dve.wait_ge(m_ready[2], hf[2] + j)
                    for t in range(NT):
                        e = dve.tensor_tensor_reduce(pr2[:, t * S:(t + 1) * S], M[:, 1, t * S:(t + 1) * S],
                                                     win[:, j % 2, P - t * P:P - t * P + S], 1.0, -3.0e38,
                                                     ALU.add, ALU.max, mxp[:, 0, t:t + 1])
                    e.then_inc(m_read[1], 1)
                    dve.wait_ge(m_read[1], hr[1] + j + 1)
                    dve.tensor_scalar(nmx[:, :, j], mxp[:, 0, :], -1.0, None, ALU.mult).then_inc(max_done, 1)
                j = i - 2
                if 0 <= j < NH2:
                    dve.wait_ge(m_ready[2], hf[2] + j + 1)
                    if j:
                        dve.wait_ge(m_ready[3], hf[3] + j)
                    dve.tensor_copy(pT2[:, :], M[:, 2, :]).then_inc(m_read[2], 1)
                j = i - 3
                if 0 <= j < NH2:
                    dve.wait_ge(m_ready[3], hf[3] + j + 1)
                    dve.tensor_copy(oraw[:, :, j * HD:(j + 1) * HD],
                                    M[:, 3, 0:2 * HD].rearrange("p (t d) -> p t d", t=NT))\
                       .then_inc(m_read[3], 1)

            def combine():
                groups = lambda ap: ap.rearrange("p t (g h) -> p t g h", g=G3)
                nm, sm = groups(nmx[:, :, :]), groups(rs[:, :, :])
                low = cmb[:, 0, 0:NT * H8].rearrange("p (t h) -> p t h", t=NT)
                den = cmb[:, 3, 0:NT * H8].rearrange("p (t h) -> p t h", t=NT)
                c_in, c_e = (cmb[:, n, :].rearrange("p (t g h) -> p t g h", t=NT, g=G3) for n in (1, 2))
                dve.wait_ge(exp_done, NH2)
                dve.wait_ge(m_read[3], hr[3] + NH2)
                link(dve.tensor_tensor(low, nm[:, :, 0, :], nm[:, :, 1, :], ALU.min))
                link(dve.tensor_tensor(low, low, nm[:, :, 2, :], ALU.min))
                for j in range(G3):
                    e = dve.tensor_tensor(c_in[:, :, j, :], low, nm[:, :, j, :], ALU.subtract)
                e.then_inc(combine_in, 1)
                dve.wait_ge(combine_exp, 1)
                link(dve.tensor_tensor(c_in, c_e, sm, ALU.mult))
                link(dve.tensor_tensor(den, c_in[:, :, 0, :], c_in[:, :, 1, :], ALU.add))
                link(dve.tensor_tensor(den, den, c_in[:, :, 2, :], ALU.add))
                link(dve.reciprocal(den, den))
                for j in range(G3):
                    e = dve.tensor_tensor(c_in[:, :, j, :], c_e[:, :, j, :], den, ALU.mult)
                e.then_inc(shares, 1)

            at = 0
            for c, (what, j) in enumerate(B2_CHUNKS):
                fill = q + B2_FILL[c]
                for k in range(2):
                    w = 2 * c + k
                    split_to(g + w + 3)
                    for _ in range(B2_STEPS[w]):
                        b2_step(at)
                        at += 1
                    if w == B2_COMBINE:
                        combine()
                    if k == 1:
                        for t in range(NT):
                            if what in ("k", "a_in"):
                                tile_ready(dve, fill, t, g + w)
                                dve.tensor_scalar(qkv[:, j % 2, 1, t, :] if what == "k" else u[:, t, :],
                                                  acc(fill, t), scaled(8, t), None, ALU.mult)\
                                   .then_inc(acc_read[fill % 2], 1)
                            elif what == "g":
                                tile_ready(dve, fill, t, g + w)
                                dve.wait_ge(b2_small, 16 * 3)
                                dve.scalar_tensor_tensor(gts[:, t, 512 * j:512 * j + 512], acc(fill, t),
                                                         rstd[:, t:t + 1], bg[:, j, :], ALU.mult, ALU.add)\
                                   .then_inc(acc_read[fill % 2], 1)
                if c == 11:
                    pf = q + B2_MIX
                    for t in range(NT):
                        tile_ready(dve, pf, t, None)
                        dve.wait_ge(acc_read[(q + B2_FILL[10]) % 2], acc_reads(q + B2_FILL[10]))
                        dve.tensor_tensor(s_a[:, t, :], acc(pf, t), s_a[:, t, :], ALU.mult)\
                           .then_inc(acc_read[pf % 2], 1)
                if c == 13:
                    pf = q + B2_YAT
                    for k in range(4):
                        if k % 2 == 0:
                            dve.wait_ge(oh_done, OH["b2"] + k + 2)
                        e = dve.scalar_tensor_tensor(yal[:, k, :],
                                                     acc(pf, k // 2)[:, (k % 2) * S:(k % 2 + 1) * S],
                                                     gains[:, G_POOL + k:G_POOL + k + 1],
                                                     yah[:, k, :].bitcast(F32), ALU.mult, ALU.subtract)
                        if k % 2:
                            e.then_inc(acc_read[pf % 2], 1)
                if c == 14:
                    pf = q + B2_YBT
                    for b in range(2):
                        dve.wait_ge(oh_done, OH["b2"] + 4 + b + 1)
                        dve.tensor_tensor(ybl[:, 2 * b:2 * b + 2, :], pair(acc(pf, b)),
                                          ybh[:, 2 * b:2 * b + 2, :].bitcast(F32), ALU.subtract)\
                           .then_inc(acc_read[pf % 2], 1)
            split_to(g + 36)
            for t in range(NT):
                for n in range(2):
                    tile_ready(dve, q + B2_PA + n, t, g + 33)
                    dve.wait_ge(gate_done, 2 * 4)
                    dve.tensor_tensor(mg[:, t, 512 * n:512 * n + 512], acc(q + B2_PA + n, t),
                                      gts[:, t, 512 * n:512 * n + 512], ALU.mult)\
                       .then_inc(acc_read[(q + B2_PA + n) % 2], 1)
                split_to(g + 37 + t)
            for t in range(NT):
                for n in range(2):
                    fill = q + B2_PB + n
                    tile_ready(dve, fill, t, g + 35)
                    cols = slice(512 * n, 512 * n + 512)
                    dve.tensor_tensor(orev[:, n, :], acc(fill, t), gts[:, t, D + 512 * n:D + 512 * n + 512],
                                      ALU.mult).then_inc(acc_read[fill % 2], 1)
                    dve.wait_ge(acc_read[fill % 2], acc_reads(fill) - 1 + t)
                    e = dve.tensor_tensor(mg[:, t, cols], mg[:, t, cols], orev[:, n, :], ALU.add)
                e.then_inc(mg_done, 1)
                split_to(g + 39 + t)
                for b in (2 * t, 2 * t + 1):
                    dve.wait_ge(oh_done, OH["b2"] + 6 + b + 1)
                    dve.tensor_tensor(xl[:, b % 2::2, t * P:(t + 1) * P],
                                      M[:, b, :].rearrange("p (k n) -> p k n", k=4),
                                      xh[:, b % 2::2, t * P:(t + 1) * P].bitcast(F32), ALU.subtract)\
                       .then_inc(m_read[b], 1)
            dve.wait_ge(fg_in, 16)
            for t in range(NT):
                residual(q + B2_OUT, g + 39, 1.0, t)
            for t in range(NT):
                dve.scalar_tensor_tensor(hn[:, t, :], h[:, t, :], scaled(9, t), fg[:, :],
                                         ALU.mult, ALU.mult).then_inc(y_done, 1)

        @block.gpsimd
        def _(pool):
            steps = [0]

            def link(ins):
                steps[0] += 1
                ins.then_inc(p_step, 1)
                pool.wait_ge(p_step, steps[0])

            def inverse_rms(dst, src, n, width, signal):
                link(pool.tensor_scalar(dst, src, 1.0 / width, EPS, ALU.mult, ALU.add))
                pool.tensor_tensor(dst, dst, mhalf[:, 0:n], ALU.pow).then_inc(signal, 1)

            def norm(r):
                for t in range(NT):
                    pool.wait_ge(sq_done, NT * r + t + 1)
                    inverse_rms(rstd[:, t:t + 1], ssq[:, t:t + 1], 1, D, rstd_done)

            link(pool.memset(mhalf[:, :], -0.5))
            pool.dma_start(flip[:, :], I["c_mats"][1]).then_inc(small_in, 16)
            pool.dma_start(tri[:, :], I["c_mats"][2]).then_inc(small_in, 16)
            pool.dma_start(causal_f[:, :], I["c_mats"][3]).then_inc(small_in, 16)
            pool.dma_start(onehot[:, :], I["c_onehot"]).then_inc(small_in, 16)
            pool.dma_start(rb[0:32, :], I["rel_bias_2"]).then_inc(small_in, 16)
            pool.dma_start(hraw[:, :], I["head_gains"]).then_inc(small_in, 16)
            pool.dma_start(rgain[:, :, :], bass.AP(I["rope_gains"].tensor, 0, [[0, P], [ROPE, 2], [1, ROPE]]))\
               .then_inc(small_in, 16)
            pool.dma_start(bf[:, :], bass.AP(I["fox_b_f"].tensor, 0, [[0, P], [1, H]])).then_inc(small_in, 16)
            pool.dma_start(freq[:, :], bass.AP(I["c_freq"].tensor, 0, [[0, P], [1, 16]])).then_inc(small_in, 16)
            pool.dma_start(posi[:, :], I["pos"]).then_inc(small_in, 16)
            norm(0)
            norm(1)
            for n, (c, width) in enumerate(((1, KVR), (0, QR))):
                for t in range(NT):
                    pool.wait_ge(lat_sq, 2 * t + 2 if n == 0 else 2 * NT + t + 1)
                    inverse_rms(lrs[:, c, t:t + 1], lss[:, c, t:t + 1], 1, width, lat_rstd)
            for n in range(2 * NT):
                c, t = n // NT, n % NT
                pool.wait_ge(heads_ss, n + 1)
                inverse_rms(hrs[:, 2 + t, 8 * c:8 * c + 8], hss[:, 2 + t, 8 * c:8 * c + 8], 8, DQ, heads_rstd)
            for c in range(2):
                for t in range(NT):
                    for n in range(2):
                        fill = PLAN["mla"][1] + 6 + 2 * c + n
                        pool.wait_ge(acc_read[fill % 2], acc_reads(fill))
                    qv = qn[:, t, :].rearrange("p (h d) -> p h d", d=DQ)[:, 8 * c:8 * c + 8]
                    tb = [tab[:, 0, t, j, :].unsqueeze(1).to_broadcast([P, 8, 16]) for j in range(4)]
                    x1, x2 = qv[:, :, NOPE:NOPE + 16], qv[:, :, NOPE + 16:DQ]
                    pool.wait_ge(heads_sq, 2 * NT + 2 * c + t + 1)
                    m4 = [rt[:, 2 * t + m // 2, 8 * (m % 2):8 * (m % 2) + 8, :] for m in range(4)]
                    for m, (x, j) in enumerate(((x1, 0), (x2, 1), (x1, 2), (x2, 3))):
                        e = pool.tensor_tensor(m4[m], x, tb[j], ALU.mult)
                    link(e)
                    pool.tensor_tensor(x1, m4[0], m4[1], ALU.subtract)
                    e = pool.tensor_tensor(x2, m4[2], m4[3], ALU.add)
                    if t:
                        e.then_inc(q_rotated, 1)
                    else:
                        link(e)
                for t in range(NT):
                    pool.wait_ge(heads_ss, 2 * NT + 2 * c + t + 1)
                    inverse_rms(hrs[:, t, 8 * c:8 * c + 8], hss[:, t, 8 * c:8 * c + 8], 8, DQ, heads_rstd)
            pool.wait_ge(m_ready[3], PLAN["n2"][2][3])
            pool.wait_ge(table_out, 16)
            pool.dma_start(p_n[:, :, :], I["p"][0, 0].rearrange("(t p) n -> p t n", p=P)).then_inc(p_in, 16)
            for r in range(2, 6):
                norm(r)
            for c in range(4):
                for t in range(NT):
                    pool.wait_ge(heads_ss, 8 + 2 * c + t + 1)
                    o = hrs[:, t, 8 * (c % 2):8 * (c % 2) + 8]
                    link(pool.tensor_scalar(o, hss[:, t, 8 * (c % 2):8 * (c % 2) + 8], 1.0 / HD, EPS,
                                            ALU.mult, ALU.add))
                    link(pool.tensor_tensor(o, o, mhalf[:, 0:8], ALU.pow))
                    pool.tensor_scalar(o, o, rstd[:, t:t + 1], None, ALU.mult).then_inc(heads_rstd, 1)
            pool.wait_ge(m_ready[3], PLAN["n6"][2][3])
            pool.dma_start(p_n[:, :, :], I["p"][1, 0].rearrange("(t p) n -> p t n", p=P)).then_inc(p_in, 16)
            for r in range(6, 9):
                norm(r)

            q = PLAN["b2"][1]
            hr = HEADS["b2"][1]
            pool.wait_ge(h_added, 2 * NT)
            pool.dma_start(bands[:, :, :, :], I["c_bands"]).then_inc(b2_small, 16)
            pool.dma_start(wp[:, :, :], I["w_pool_2"][0].rearrange("g c d -> c g d")).then_inc(b2_small, 16)

            pool.dma_start(bg[:, :, :], bass.AP(I["b_gate_2"].tensor, 0, [[0, P], [512, 4], [1, 512]]))\
                .then_inc(b2_small, 16)
            pool.wait_ge(table_out, 16)
            for j in range(NH2):
                if j >= 2:
                    pool.wait_ge(m_read[1], hr[1] + j - 1)
                pool.dma_start(win[:, j % 2, :], bass.AP(scratch, 512 * j, [[1, P], [1, WIN]]))\
                    .then_inc(win_in[j % 2], 16)
            pool.wait_ge(m_ready[3], HEADS["b2"][0][3] + NH2)
            pool.dma_start(fg[:, :], bass.AP(I["final_gain_2"].tensor, 0, [[0, P], [1, D]])).then_inc(fg_in, 16)

            c_in = cmb[:, 1, :].rearrange("p (t g h) -> p t g h", t=NT, g=G3)
            pool.wait_ge(shares, 1)
            for j in range(G3):
                dst = orev if j == 0 else otmp
                for t in range(NT):
                    e = pool.tensor_tensor(dst[:, t, :].rearrange("p (h d) -> p h d", d=HD),
                                           oraw[:, t, 512 * j:512 * j + 512].rearrange("p (h d) -> p h d", d=HD),
                                           c_in[:, t, j, :].unsqueeze(2).to_broadcast([P, H8, HD]), ALU.mult)
                link(e)
                if j:
                    link(pool.tensor_tensor(orev[:, :, :], orev[:, :, :], otmp[:, :, :], ALU.add))
            fill = q + B2_PERM
            pool.wait_ge(acc_read[fill % 2], acc_reads(fill))
            pool.tensor_tensor(orev[:, :, :], orev[:, :, :],
                               s_b[:, :, :], ALU.mult).then_inc(o_done, 1)
            norm(9)


def constants():
    i = np.arange(P)
    mats = np.zeros((4, P, P), np.float32)
    mats[0] = np.eye(P)
    mats[1] = np.eye(P)[::-1]
    mats[2] = i[:, None] <= i[None, :]
    mats[3] = np.where(i[None, :] > i[:, None], np.float32(NEG), np.float32(0))
    onehot = np.zeros((33, G3, 512), np.float32)
    for g, (window, dil) in enumerate(DILATED):
        for m in range(512):
            off = m - (S - 1)
            n = abs(off)
            if off % dil or n > window // 2:
                onehot[32, g, m] = 1
                continue
            large = 8 + int(np.float32(np.log(np.float32(max(n, 1)) / np.float32(8)) / np.float32(np.log(128.0)) * 8))
            onehot[(16 if off > 0 else 0) + (n if n < 8 else min(large, 15)), g, m] = 1
    bands = np.zeros((P, NT, 4, S), np.float32)
    for g, w in enumerate(POOL_WINDOWS):
        for t in range(S):
            lo, hi = max(t - w // 2, 0), min(t + w // 2 - 1, S - 1)
            for s in range(lo, hi + 1):
                bands[s % P, s // P, g, t] += np.float32(1) / np.float32(hi - lo + 1)
            bands[t % P, t // P, g, t] -= 1
    freq = (np.float32(10000.0) ** (-np.arange(0, ROPE, 2, dtype=np.float32) / ROPE)).astype(np.float32)
    return {"c_mats": mats, "c_onehot": onehot.reshape(33, G3 * 512), "c_bands": bands, "c_freq": freq}


_AS_IS = ["x", "p", "ffn1_w_in", "ffn1_w_out", "ffn2_w_in", "ffn2_w_out", "ple_w_proj", "ple_w_gate", "mla_w_in",
          "mla_w_uq", "mla_w_ukv", "mla_w_o", "fox_w_in", "fox_b_f", "fox_w_o", "w_in_2", "b_gate_2",
          "rel_bias_2", "w_pool_2", "w_proj_a_2", "w_proj_b_2", "w_out_2", "final_gain_2"]
_OUTS = [((1, S, D), "float32")]


def kernel(**inputs):
    import concourse.bacc as _bacc
    from concourse.bass_utils import run_bass_kernel_spmd as _run

    def per_feature(v):
        return np.asarray(v).reshape(-1, P).T

    arrays = {n: np.ascontiguousarray(inputs[n]) for n in _AS_IS}
    arrays["gains"] = np.ascontiguousarray(np.concatenate(
        [per_feature(inputs[n][i]) for i in range(2) for n in ("g_ffn1", "g_mix", "g_ffn2", "g_ple")]
        + [per_feature(inputs[n]) for n in ("mla_g_q_lat", "mla_g_kv_lat", "norm_gain_2", "pool_scale_2")], axis=1))
    arrays["head_gains"] = np.ascontiguousarray(np.stack(
        [np.asarray(inputs[n])[0, :HD] for n in ("mla_g_qn", "mla_g_kn", "fox_g_qn", "fox_g_kn")], axis=1))
    arrays["rope_gains"] = np.ascontiguousarray(np.stack(
        [np.asarray(inputs[n])[0, NOPE:] for n in ("mla_g_qn", "mla_g_kn")]))
    arrays["pos"] = np.ascontiguousarray(np.asarray(inputs["positions"])[0].reshape(NT, P).T)
    arrays.update(constants())

    nc = _bacc.Bacc("TRN2", target_bir_lowering=False, num_devices=1)
    feed, I = {}, {}
    for name, a in arrays.items():
        feed[f"in_{name}_dram"] = a
        I[name] = nc.dram_tensor(f"in_{name}_dram", a.shape, mybir.dt.from_np(a.dtype), kind="ExternalInput").ap()
    out = nc.dram_tensor("out_0_dram", _OUTS[0][0], F32, kind="ExternalOutput").ap()
    build(nc, I, out)
    r = _run(nc, [feed], core_ids=[0])
    return r.results[0]["out_0_dram"]
```
